# Optimizing a Trainium2 kernel written in Bass

```python
import jax, jax.numpy as jnp
from jax import lax
import numpy as np

D_MODEL = 1024
BATCH = 1
SEQ = 256
DEPTH = 2

D_CONF = 512
CONF_KERNEL = 31
D_SHORT = 512
SHORT_KERNEL = 3
D_FF_DENSE = 2816
N_EXPERTS = 8
TOP_K = 2
D_FF_EXPERT = 3584
RMS_EPS = 1e-6
LN_EPS = 1e-5
IN_COLS = 2 * D_CONF + 3 * D_SHORT + 2 * D_MODEL

kernel_name = "hybrid_conformer_shortconv_moe_trunk"

def rmsnorm(x, g):
    xf = x.astype(jnp.float32)
    y = xf * lax.rsqrt(jnp.mean(xf * xf, axis=-1, keepdims=True) + RMS_EPS)
    return (y * g.astype(jnp.float32)).astype(x.dtype)

def layernorm(x, g, b):
    xf = x.astype(jnp.float32)
    mu = jnp.mean(xf, axis=-1, keepdims=True)
    var = jnp.mean(jnp.square(xf - mu), axis=-1, keepdims=True)
    y = (xf - mu) * lax.rsqrt(var + LN_EPS)
    return (y * g.astype(jnp.float32) + b.astype(jnp.float32)).astype(x.dtype)

def causal_dwconv(x, w):
    k, c = w.shape
    return lax.conv_general_dilated(
        x, w[:, None, :].astype(x.dtype), window_strides=(1,), padding=[(k - 1, 0)],
        dimension_numbers=("NWC", "WIO", "NWC"), feature_group_count=c)

def token_mixer(h, w_in, conv_a, conv_a_bias, ln_a_g, ln_a_b, w_a, conv_b, w_b, w_o):
    z = h @ w_in
    splits = np.cumsum([D_CONF, D_CONF, D_SHORT, D_SHORT, D_SHORT, D_MODEL]).tolist()
    a_val, a_gate, s_b, s_c, s_x, g_a, g_b = jnp.split(z, splits, axis=-1)
    a = a_val * jax.nn.sigmoid(a_gate)
    a = causal_dwconv(a, conv_a) + conv_a_bias
    a = jax.nn.silu(layernorm(a, ln_a_g, ln_a_b))
    y_a = a @ w_a
    u = causal_dwconv(s_c * s_x, conv_b)
    y_b = (s_b * u) @ w_b
    merged = jax.nn.sigmoid(g_a) * y_a + jax.nn.sigmoid(g_b) * y_b
    return merged @ w_o

def swiglu(h, w1, w3, w2):
    return (jax.nn.silu(h @ w1) * (h @ w3)) @ w2

def moe_ffn(h, router, we1, we3, we2):
    logits = (h @ router).astype(jnp.float32)
    top_vals, top_idx = lax.top_k(logits, TOP_K)
    top_w = jax.nn.softmax(top_vals, axis=-1)
    combine = jnp.sum(jax.nn.one_hot(top_idx, N_EXPERTS, dtype=jnp.float32) * top_w[..., None], axis=-2)
    combine = combine.astype(h.dtype)
    out = jnp.zeros_like(h)
    for e in range(N_EXPERTS):
        out = out + combine[..., e:e + 1] * swiglu(h, we1[e], we3[e], we2[e])
    return out

def setup_inputs(seed: int = 0) -> dict:
    key = jax.random.key(seed)
    keys = iter(jax.random.split(key, 64))
    nrm = lambda shape, scale: jax.random.normal(next(keys), shape, jnp.float32) * scale
    gain = lambda n: 1.0 + nrm((n,), 0.02)
    inp = {"x": nrm((BATCH, SEQ, D_MODEL), 1.0)}
    for l in range(DEPTH):
        p = f"l{l}_"
        inp[p + "norm1"] = gain(D_MODEL)
        inp[p + "w_in"] = nrm((D_MODEL, IN_COLS), D_MODEL ** -0.5)
        inp[p + "conv_a"] = nrm((CONF_KERNEL, D_CONF), CONF_KERNEL ** -0.5)
        inp[p + "conv_a_bias"] = nrm((D_CONF,), 0.02)
        inp[p + "ln_a_g"] = gain(D_CONF)
        inp[p + "ln_a_b"] = nrm((D_CONF,), 0.02)
        inp[p + "w_a"] = nrm((D_CONF, D_MODEL), D_CONF ** -0.5)
        inp[p + "conv_b"] = nrm((SHORT_KERNEL, D_SHORT), SHORT_KERNEL ** -0.5)
        inp[p + "w_b"] = nrm((D_SHORT, D_MODEL), D_SHORT ** -0.5)
        inp[p + "w_o"] = nrm((D_MODEL, D_MODEL), D_MODEL ** -0.5)
        inp[p + "norm2"] = gain(D_MODEL)
        if l % 2 == 0:
            inp[p + "ffn_w1"] = nrm((D_MODEL, D_FF_DENSE), D_MODEL ** -0.5)
            inp[p + "ffn_w3"] = nrm((D_MODEL, D_FF_DENSE), D_MODEL ** -0.5)
            inp[p + "ffn_w2"] = nrm((D_FF_DENSE, D_MODEL), D_FF_DENSE ** -0.5)
        else:
            inp[p + "router"] = nrm((D_MODEL, N_EXPERTS), D_MODEL ** -0.5)
            inp[p + "moe_w1"] = nrm((N_EXPERTS, D_MODEL, D_FF_EXPERT), D_MODEL ** -0.5)
            inp[p + "moe_w3"] = nrm((N_EXPERTS, D_MODEL, D_FF_EXPERT), D_MODEL ** -0.5)
            inp[p + "moe_w2"] = nrm((N_EXPERTS, D_FF_EXPERT, D_MODEL), D_FF_EXPERT ** -0.5)
    inp["final_norm"] = gain(D_MODEL)
    return inp

def reference(x,
              l0_norm1, l0_w_in, l0_conv_a, l0_conv_a_bias, l0_ln_a_g, l0_ln_a_b, l0_w_a, l0_conv_b, l0_w_b, l0_w_o,
              l0_norm2, l0_ffn_w1, l0_ffn_w3, l0_ffn_w2,
              l1_norm1, l1_w_in, l1_conv_a, l1_conv_a_bias, l1_ln_a_g, l1_ln_a_b, l1_w_a, l1_conv_b, l1_w_b, l1_w_o,
              l1_norm2, l1_router, l1_moe_w1, l1_moe_w3, l1_moe_w2,
              final_norm):
    mixer_params = [
        (l0_w_in, l0_conv_a, l0_conv_a_bias, l0_ln_a_g, l0_ln_a_b, l0_w_a, l0_conv_b, l0_w_b, l0_w_o),
        (l1_w_in, l1_conv_a, l1_conv_a_bias, l1_ln_a_g, l1_ln_a_b, l1_w_a, l1_conv_b, l1_w_b, l1_w_o),
    ]
    norm1 = [l0_norm1, l1_norm1]
    norm2 = [l0_norm2, l1_norm2]
    dense_params = [(l0_ffn_w1, l0_ffn_w3, l0_ffn_w2)]
    moe_params = [(l1_router, l1_moe_w1, l1_moe_w3, l1_moe_w2)]
    for layer in range(DEPTH):
        x = x + token_mixer(rmsnorm(x, norm1[layer]), *mixer_params[layer])
        h = rmsnorm(x, norm2[layer])
        if layer % 2 == 0:
            x = x + swiglu(h, *dense_params[layer // 2])
        else:
            x = x + moe_ffn(h, *moe_params[layer // 2])
    return rmsnorm(x, final_norm)


_drawn_inputs = setup_inputs


def setup_inputs(seed=0):
    import zlib

    import numpy as np

    out = dict(_drawn_inputs(seed))
    spreads = {}
    factors = {'l0_ln_a_g': 4.146,
     'l0_ln_a_b': 10.0,
     'l1_conv_a_bias': 4.214,
     'l1_ln_a_g': 13.762,
     'l1_ln_a_b': 64.0,
     'final_norm': 21.239,
     'l0_norm2': 4.213,
     'l1_norm2': 4.19,
     'l1_norm1': 2.965}
    for name, (base, spread) in spreads.items():
        noise = np.random.default_rng([zlib.crc32(name.encode()), seed]).standard_normal(out[name].shape)
        drawn = base * np.exp(spread * noise) if base else spread * noise
        out[name] = __import__('jax').numpy.asarray(drawn.astype(out[name].dtype))
    for name, factor in factors.items():
        out[name] = (out[name] * factor).astype(out[name].dtype)
    return out
```

```python
from contextlib import ExitStack

import concourse.bass as bass
from concourse import mybir

F32 = mybir.dt.float32
F32R = mybir.dt.float32r
I32 = mybir.dt.int32
ALU = mybir.AluOpType
ACT = mybir.ActivationFunctionType
AX = mybir.AxisListType

P = 128
BANK = 512
UNIT = 2048
RAW_SLOTS = 6
SPLIT_SLOTS = 3
RMS_EPS = 1e-6
LN_EPS = 1e-5


class Unit:

    def __init__(self, fixed, item=0, step=0):
        self.n = item * 42 + step * 6 + fixed
        self.first_round = fixed < SPLIT_SLOTS
        self.first_raw_round = fixed < RAW_SLOTS
        self.raw = fixed % RAW_SLOTS
        self.split = fixed % SPLIT_SLOTS
        self.loads = item * 7 + step + (fixed // RAW_SLOTS + 1)


def trunk(nc, ins, out):
    x_in = ins["x"]
    _, SEQ, D = x_in.shape
    TT = SEQ // P
    KD = D // P
    KA, C = ins["l0_conv_a"].shape
    KB, CS = ins["l0_conv_b"].shape
    NC = C // P
    FD = ins["l0_ffn_w1"].shape[1]
    E, _, FE = ins["l1_moe_w1"].shape
    assert TT == 2 and KD == 8 and NC == 4 and CS == C == BANK and D == 2 * BANK
    MOE_CHUNKS = FE // BANK
    assert MOE_CHUNKS == 7 and FE % BANK == 0
    DENSE_CHUNKS = FD // BANK
    assert FD == DENSE_CHUNKS * BANK + BANK // 2

    A_VAL, A_GATE, S_C, S_X, S_B, G0 = range(6)
    z_cols = [0, C, 2 * C + CS, 2 * C + 2 * CS, 2 * C] + [2 * C + 3 * CS + BANK * j for j in range(4)]
    NZ = len(z_cols)
    U_WB = 2 * NZ
    U_WA = U_WB + 2
    U_WO = U_WA + 2
    MIX_UNITS = U_WO + 4
    FFN_UNITS = 6 * DENSE_CHUNKS + 3
    LAYER_UNITS = MIX_UNITS + FFN_UNITS
    MOE0 = LAYER_UNITS + MIX_UNITS
    BIAS, LNG, LNB, CONVB = (KA * NC + NC * j for j in range(4))
    NPAR = CONVB + KB * NC
    GDENSE = TT * (DENSE_CHUNKS + 1)

    def rows(w, k):
        return w.rearrange("(k p) n -> p k n", p=P)[:, k[0]:k[1], :]

    def layer_units(l):
        w_in = ins[f"l{l}_w_in"]
        out_ = [rows(w_in, (4 * u, 4 * u + 4))[:, :, c:c + BANK] for c in z_cols for u in range(2)]
        for name, tiles in (("w_b", NC), ("w_a", NC), ("w_o", KD)):
            out_ += [rows(ins[f"l{l}_{name}"], (j, j + 2)) for j in range(0, tiles, 2)]
        return out_

    def dense_units():
        w1, w3, w2 = (ins[f"l0_ffn_{n}"] for n in ("w1", "w3", "w2"))
        out_ = []
        for c in range(DENSE_CHUNKS):
            for w in (w1, w3):
                out_ += [rows(w, (4 * u, 4 * u + 4))[:, :, BANK * c:BANK * (c + 1)] for u in range(2)]
            if c:
                out_ += [rows(w2, (4 * (c - 1) + 2 * u, 4 * (c - 1) + 2 * u + 2)) for u in range(2)]
        last = BANK * DENSE_CHUNKS
        out_ += [rows(w, (0, KD))[:, :, last:FD] for w in (w1, w3)]
        out_ += [rows(w2, (4 * DENSE_CHUNKS - 4 + 2 * u, 4 * DENSE_CHUNKS - 2 + 2 * u)) for u in range(2)]
        out_ += [rows(w2, (4 * DENSE_CHUNKS, FD // P))]
        return out_

    static_units = layer_units(0) + dense_units() + layer_units(1)
    assert len(static_units) == MOE0
    moe_up = [ins[f"l1_moe_{n}"].rearrange("e (k p) f -> e p k f", p=P) for n in ("w1", "w3")]
    moe_down = ins["l1_moe_w2"].rearrange("e (k p) n -> e p k n", p=P)

    with ExitStack() as ctx:
        def sb(name, shape, dt=F32):
            return ctx.enter_context(nc.sbuf_tensor(name, [P] + shape, dt))

        def sem(name):
            return ctx.enter_context(nc.semaphore(name))

        raw = [sb(f"raw{s}", [UNIT]) for s in range(RAW_SLOTS)]
        w_hi = [sb(f"w_hi{s}", [UNIT], F32R) for s in range(SPLIT_SLOTS)]
        w_lo = [sb(f"w_lo{s}", [UNIT], F32R) for s in range(SPLIT_SLOTS)]
        x = sb("x", [TT, D])
        h = sb("h", [TT, D])
        gates = sb("gates", [TT, 2 * D])
        a_tok = sb("a_tok", [TT, BANK])
        v_tok = sb("v_tok", [TT, BANK])
        b_tok = sb("b_tok", [TT, BANK])
        actT_hi = sb("actT_hi", [KD, SEQ], F32R)
        actT_lo = sb("actT_lo", [KD, SEQ], F32R)
        branch_hi = [sb(f"branch_hi{b}", [NC, SEQ], F32R) for b in range(2)]
        branch_lo = [sb(f"branch_lo{b}", [NC, SEQ], F32R) for b in range(2)]
        convin_a = sb("convin_a", [NC, KA - 1 + SEQ])
        convin_b = sb("convin_b", [NC, KB - 1 + SEQ])
        conv_a = sb("conv_a", [NC, SEQ])
        conv_b = sb("conv_b", [NC, SEQ])
        tap = sb("tap", [SEQ])
        ln_sd = sb("ln_sd", [SEQ])
        ln_rstd = sb("ln_rstd", [SEQ])
        params_in = [[sb(f"params_in{l}{j}", [P]) for j in range(2)] for l in range(2)]
        params = [sb(f"params{l}", [NPAR]) for l in range(2)]
        gain = sb("gain", [D])
        ident = sb("ident", [P])
        mean_of = sb("mean_of", [P])
        ones = sb("ones", [P])
        before = sb("before", [P])
        sumsq = sb("sumsq", [10])
        rstd = sb("rstd", [10])
        newton = sb("newton", [10])
        ln_eps = sb("ln_eps", [1])
        router = sb("router", [KD, E])
        router_hi = sb("router_hi", [KD, E], F32R)
        router_lo = sb("router_lo", [KD, E], F32R)
        earlier = sb("earlier", [E, E])
        iota_e = sb("iota_e", [E])
        iota_s = sb("iota_s", [SEQ])
        logits = sb("logits", [TT, E])
        pair_gt = sb("pair_gt", [TT, E, E])
        pair_eq = sb("pair_eq", [TT, E, E])
        rank = sb("rank", [TT, E])
        chosen = sb("chosen", [TT, E])
        top = sb("top", [TT])
        prob = sb("prob", [TT, E])
        total = sb("total", [TT])
        route = sb("route", [E, 2 * TT])
        place = sb("place", [TT, E])
        over = sb("over", [E])
        over_before = sb("over_before", [E])
        over_pairs = sb("over_pairs", [E, E])
        over_index = sb("over_index", [E])
        items_f = sb("items_f", [1 + 2 * E])
        items = sb("items", [1 + 2 * E], I32)
        cur = sb("cur", [2 * TT])
        cur_weight = sb("cur_weight", [TT])
        sel = sb("sel", [TT, P])
        selT = sb("selT", [SEQ])
        silu = gates
        g_tok = a_tok
        gT_hi, gT_lo = branch_hi[0], branch_lo[0]
        y_sb = v_tok

        ps = ctx.enter_context(nc.psum_tensor("ps", [P, 8, BANK], F32))

        raw_landed = [sem(f"raw_landed{s}") for s in range(RAW_SLOTS)]
        unit_hi = sem("unit_hi")
        unit_lo = sem("unit_lo")
        unit_done = sem("unit_done")
        params_landed = sem("params_landed")
        x_landed = sem("x_landed")
        router_landed = sem("router_landed")
        gain_landed = sem("gain_landed")
        pool_step = sem("pool_step")
        consts_ready = sem("consts_ready")
        pads_ready = sem("pads_ready")
        paramsT_done = sem("paramsT_done")
        params_ready = sem("params_ready")
        sumsq_ready = sem("sumsq_ready")
        h_ready = sem("h_ready")
        tT_done = sem("tT_done")
        tT_hi = sem("tT_hi")
        tT_lo = sem("tT_lo")
        sig_ready = sem("sig_ready")
        a_ready = sem("a_ready")
        aT_done = sem("aT_done")
        convin_a_ready = sem("convin_a_ready")
        c_ready = sem("c_ready")
        v_ready = sem("v_ready")
        vT_done = sem("vT_done")
        convin_b_ready = sem("convin_b_ready")
        b_ready = sem("b_ready")
        bT_done = sem("bT_done")
        gate_ready = sem("gate_ready")
        conv_a_dve = sem("conv_a_dve")
        conv_a_pool = sem("conv_a_pool")
        conv_b_pool = sem("conv_b_pool")
        ub_ready = sem("ub_ready")
        branch_hi_ready = [sem(f"branch_hi_ready{b}") for b in range(2)]
        branch_lo_ready = [sem(f"branch_lo_ready{b}") for b in range(2)]
        mean_done = sem("mean_done")
        centred = sem("centred")
        squares_ready = sem("squares_ready")
        var_done = sem("var_done")
        ln_sd_ready = sem("ln_sd_ready")
        normed = sem("normed")
        lnsilu_ready = sem("lnsilu_ready")
        ya_tile0_done = sem("ya_tile0_done")
        merged_ready = sem("merged_ready")
        res_tile0_done = sem("res_tile0_done")
        x_ready = sem("x_ready")
        dve_step = sem("dve_step")
        silu_ready = sem("silu_ready")
        g_ready = sem("g_ready")
        gT_done = sem("gT_done")
        gT_hi_ready = sem("gT_hi_ready")
        gT_lo_ready = sem("gT_lo_ready")
        router_hi_ready = sem("router_hi_ready")
        router_ready = sem("router_ready")
        logits_done = sem("logits_done")
        shifted_ready = sem("shifted_ready")
        exp_ready = sem("exp_ready")
        chosen_ready = sem("chosen_ready")
        count_done = sem("count_done")
        items_ready = sem("items_ready")
        cur_ready = sem("cur_ready")
        sel_ready = sem("sel_ready")
        gather_done = sem("gather_done")
        selT_done = sem("selT_done")
        selT_ready = sem("selT_ready")
        hsel_hi_ready = sem("hsel_hi_ready")
        hsel_lo_ready = sem("hsel_lo_ready")
        y_copied = sem("y_copied")
        scatter_done = sem("scatter_done")
        stored = sem("stored")

        RESIDUALS = 3
        scatter_banks = ((2, 3), (5, 7))

        block = ctx.enter_context(nc.Block())

        def moe_unit(kind, i, c, u):
            if kind != "down":
                at = u + (0 if kind == "w1" else 2)
                return Unit(MOE0 + at, i) if isinstance(c, int) and c == 0 else Unit(MOE0 - 2 + at, i, c)
            if isinstance(c, int) and c == MOE_CHUNKS:
                return Unit(MOE0 + 6 * MOE_CHUNKS - 2 + u, i)
            return Unit(MOE0 + 2 + u, i, c)

        def items_of(eng):
            eng.wait_ge(items_ready, 1)
            return eng.value_load(items[0:1, 0:1], min_val=E, max_val=2 * E)

        def for_items(eng, start, body, prepared):
            start(0, prepared)
            with eng.Fori(0, E - 1) as i:
                body(i, lambda: (i + 1, i + 1, 0))
            body(E - 1, None)
            n = items_of(eng)
            with eng.If(n > E):
                with eng.Fori(E, n) as i:
                    start(i, 0)
                    body(i, None)
            return n

        @block.sync
        def _(eng):
            def load(u, src):
                if not u.first_raw_round:
                    eng.wait_ge(unit_lo, u.n - (RAW_SLOTS - 1))
                k = src.shape[1]
                dst = raw[u.raw][:, 0:k * src.shape[2]].rearrange("p (k n) -> p k n", k=k)
                eng.dma_start(dst, src).then_inc(raw_landed[u.raw], 16)

            x_rows = x_in.rearrange("b (t p) d -> p (b t) d", p=P)
            eng.dma_start(x[:, :, :], x_rows).then_inc(x_landed, 16)
            for n, src in enumerate(static_units):
                load(Unit(n), src)

            def item(i, e):
                def up(c):
                    for w, kind in zip(moe_up, ("w1", "w3")):
                        for u in range(2):
                            cols = slice(0, BANK) if isinstance(c, int) else bass.ds(c * BANK, BANK)
                            load(moe_unit(kind, i, c, u), w[e, :, 4 * u:4 * u + 4, cols])

                def down(c):
                    for u in range(2):
                        load(moe_unit("down", i, c, u), moe_down[e, :, bass.ds(4 * (c - 1) + 2 * u, 2), :])

                up(0)
                with eng.Fori(1, MOE_CHUNKS) as c:
                    up(c)
                    down(c)
                down(MOE_CHUNKS)

            with eng.Fori(0, E) as i:
                item(i, i)
            n = items_of(eng)
            with eng.If(n > E):
                with eng.Fori(E, n) as i:
                    item(i, eng.value_load(items[0:1, bass.ds(i + 1, 1)], min_val=0, max_val=E - 1))
            for t in range(TT):
                eng.wait_ge(h_ready, 2 * 4 + t + 1)
                eng.dma_start(out.rearrange("b (t p) d -> p (b t) d", p=P)[:, t, :],
                              h[:, t, :]).then_inc(stored, 16)
            eng.wait_ge(stored, 32)

        @block.gpsimd
        def _(eng):
            step = [0]

            def done(ins_):
                step[0] += 1
                ins_.then_inc(pool_step, 1)
                eng.wait_ge(pool_step, step[0])

            for l in range(2):
                eng.dma_start(params_in[l][0][0:KA * NC, :],
                              ins[f"l{l}_conv_a"].rearrange("k (c p) -> (k c) p", p=P)).then_inc(params_landed, 16)
                at = 0
                for name in ("conv_a_bias", "ln_a_g", "ln_a_b"):
                    eng.dma_start(params_in[l][1][at:at + NC, :],
                                  ins[f"l{l}_{name}"].rearrange("(c p) -> c p", p=P)).then_inc(params_landed, 16)
                    at += NC
                eng.dma_start(params_in[l][1][at:at + KB * NC, :],
                              ins[f"l{l}_conv_b"].rearrange("k (c p) -> (k c) p", p=P)).then_inc(params_landed, 16)
            norms = [ins[n] for n in ("l0_norm1", "l0_norm2", "l1_norm1", "l1_norm2", "final_norm")]

            def load_gain(k):
                if k:
                    eng.wait_ge(h_ready, 2 * k)
                eng.dma_start(gain[:, :], norms[k].rearrange("(a d) -> a d", a=1).to_broadcast([P, D])
                              ).then_inc(gain_landed, 16)

            load_gain(0)
            with nc.allow_non_contiguous_dma(reason="the router's rows are eight floats"):
                eng.dma_start(router[:, :, :], ins["l1_router"].rearrange("(k p) e -> p k e", p=P)
                              ).then_inc(router_landed, 16)

            done(eng.memset(ident[:, :], 0.0))
            done(eng.affine_select(out=ident[:, :], in_=ident[:, :], compare_op=ALU.not_equal, fill=1.0,
                                   base=0, pattern=[[-1, P]], channel_multiplier=1))
            done(eng.memset(before[:, :], 0.0))
            done(eng.affine_select(out=before[:, :], in_=before[:, :], compare_op=ALU.is_ge, fill=1.0,
                                   base=0, pattern=[[-1, P]], channel_multiplier=1))
            done(eng.memset(earlier[:, :, :], 0.0))
            done(eng.affine_select(out=earlier[:, :, :], in_=earlier[:, :, :], compare_op=ALU.is_ge, fill=1.0,
                                   base=0, pattern=[[-1, E], [1, E]], channel_multiplier=0))
            done(eng.iota(iota_e[:, :], [[1, E]], base=0, channel_multiplier=0, allow_small_or_imprecise_dtypes=True))
            done(eng.iota(iota_s[:, :], [[1, SEQ]], base=0, channel_multiplier=0, allow_small_or_imprecise_dtypes=True))
            eng.memset(mean_of[:, :], 1.0 / C).then_inc(consts_ready, 1)
            eng.memset(ones[:, :], 1.0).then_inc(consts_ready, 1)
            eng.memset(ln_eps[:, :], LN_EPS).then_inc(consts_ready, 1)
            eng.memset(convin_a[:, :, 0:KA - 1], 0.0).then_inc(pads_ready, 1)
            eng.memset(convin_b[:, :, 0:KB - 1], 0.0).then_inc(pads_ready, 1)
            eng.wait_ge(pads_ready, 2)

            for l in range(2):
                par = params[l]

                def one_tap(acc, src, w, signal=None):
                    done(eng.tensor_scalar(tap[:, :], src, w, None, ALU.mult))
                    add = eng.tensor_tensor(acc, acc, tap[:, :], ALU.add)
                    if signal is None:
                        done(add)
                    else:
                        add.then_inc(signal, 1)
                        eng.wait_ge(signal, l + 1)

                def taps_a(ks):
                    c = NC - 1
                    for k in ks:
                        src = convin_a[:, c, k:k + SEQ]
                        w = par[:, k * NC + c:k * NC + c + 1]
                        if k == 0:
                            done(eng.tensor_scalar(conv_a[:, c, :], src, w, par[:, BIAS + c:BIAS + c + 1],
                                                   ALU.mult, ALU.add))
                        else:
                            one_tap(conv_a[:, c, :], src, w, conv_a_pool if k == KA - 1 else None)

                load_gain(2 * l + 1)
                eng.wait_ge(params_ready, 2)
                eng.wait_ge(convin_a_ready, TT * (l + 1))
                if l:
                    eng.wait_ge(lnsilu_ready, NC * l)
                taps_a(range(KA // 2))
                eng.wait_ge(convin_b_ready, TT * (l + 1))
                if l:
                    eng.wait_ge(branch_lo_ready[1], l)
                for c in range(NC):
                    for k in range(KB):
                        w = par[:, CONVB + k * NC + c:CONVB + k * NC + c + 1]
                        if k == 0:
                            done(eng.tensor_scalar(conv_b[:, c, :], convin_b[:, c, k:k + SEQ], w, None, ALU.mult))
                        else:
                            one_tap(conv_b[:, c, :], convin_b[:, c, k:k + SEQ], w,
                                    conv_b_pool if (c, k) == (NC - 1, KB - 1) else None)
                taps_a(range(KA // 2, KA))
                load_gain(2 * l + 2)

        @block.scalar
        def _(eng):
            def hi(u):
                eng.wait_ge(raw_landed[u.raw], u.loads * 16)
                if not u.first_round:
                    eng.wait_ge(unit_done, u.n - (SPLIT_SLOTS - 1))
                nc.scalar.activation(w_hi[u.split][:, :], raw[u.raw][:, :], ACT.Copy).then_inc(unit_hi, 1)

            def norm(k, t):
                if k == 0:
                    eng.wait_ge(x_landed, 16)
                elif k < 4:
                    eng.wait_ge(x_ready, 4 * (k - 1) + 2 * t + 2)
                nc.scalar.activation(h[:, t, :], x[:, t, :], ACT.Square, scale=float(D) ** -0.5,
                                     accum_out=sumsq[:, 2 * k + t:2 * k + t + 1]).then_inc(sumsq_ready, 1)

            def transposed_hi(r, t):
                eng.wait_ge(tT_done, 2 * r + t + 1)
                for b in range(2):
                    nc.scalar.activation(actT_hi[:, 4 * b:4 * b + 4, P * t:P * t + P],
                                         ps[:, 4 + 2 * t + b, :].rearrange("p (k n) -> p k n", k=4),
                                         ACT.Copy).then_inc(tT_hi, 1)

            def norm_block(k, r, m):
                for t in range(TT):
                    norm(k, t)
                hi(Unit(m + 1))
                for t in range(TT):
                    transposed_hi(r, t)
                hi(Unit(m + 2))

            def chunk_banks(k):
                return 2 * (k % 3)

            def from_z(l, k, func, dst, ready, free=None):
                eng.wait_ge(unit_done, LAYER_UNITS * l + 2 * k + 2)
                if free is not None:
                    eng.wait_ge(*free)
                for t in range(TT):
                    last = nc.scalar.activation(dst(t), ps[:, chunk_banks(k) + t, :], func)
                    if ready is not gate_ready or t == TT - 1:
                        last.then_inc(ready, 1)

            def mixer(l):
                U = LAYER_UNITS * l
                for j in range(3, 6):
                    hi(Unit(U + j))
                from_z(l, A_GATE, ACT.Sigmoid, lambda t: gates[:, t, BANK:2 * BANK], sig_ready,
                       (g_ready, GDENSE) if l else None)
                hi(Unit(U + 6))
                hi(Unit(U + 7))
                from_z(l, S_C, ACT.Copy, lambda t: gates[:, t, 0:BANK], c_ready)
                for t in range(TT):
                    eng.wait_ge(aT_done, TT * l + t + 1)
                    if t == 0 and l == 0:
                        eng.wait_ge(pads_ready, 2)
                    if t == 0 and l:
                        eng.wait_ge(centred, l)
                    nc.scalar.activation(convin_a[:, :, KA - 1 + P * t:KA - 1 + P * t + P],
                                         ps[:, 6 + t, :].rearrange("p (c n) -> p c n", c=NC),
                                         ACT.Copy).then_inc(convin_a_ready, 1)
                for j in range(8, 12):
                    hi(Unit(U + j))
                from_z(l, S_B, ACT.Copy, lambda t: b_tok[:, t, :], b_ready)
                for t in range(TT):
                    eng.wait_ge(vT_done, TT * l + t + 1)
                    if t == 0 and l:
                        eng.wait_ge(ub_ready, TT * l)
                    nc.scalar.activation(convin_b[:, :, KB - 1 + P * t:KB - 1 + P * t + P],
                                         ps[:, 6 + t, :].rearrange("p (c n) -> p c n", c=NC),
                                         ACT.Copy).then_inc(convin_b_ready, 1)
                for k in range(G0, NZ - 1):
                    hi(Unit(U + 2 * k + 2))
                    hi(Unit(U + 2 * k + 3))
                    at = (k - G0) * BANK
                    from_z(l, k, ACT.Sigmoid, lambda t: gates[:, t, at:at + BANK], gate_ready,
                           (v_ready, TT * (l + 1)) if k == G0 else (a_ready, TT * (l + 1)))
                eng.wait_ge(ub_ready, TT * (l + 1))
                nc.scalar.activation(branch_hi[1][:, :, :], conv_b[:, :, :], ACT.Copy).then_inc(branch_hi_ready[1], 1)
                hi(Unit(U + U_WB))
                hi(Unit(U + U_WB + 1))
                eng.wait_ge(centred, l + 1)
                nc.scalar.activation(a_tok[:, :, :].rearrange("p t n -> p (t n)"),
                                     conv_a[:, :, :].rearrange("p c n -> p (c n)"),
                                     ACT.Square).then_inc(squares_ready, 1)
                at3 = 3 * BANK
                from_z(l, NZ - 1, ACT.Sigmoid, lambda t: gates[:, t, at3:at3 + BANK], gate_ready)
                hi(Unit(U + U_WA))
                hi(Unit(U + U_WA + 1))
                eng.wait_ge(var_done, l + 1)
                eng.wait_ge(consts_ready, 3)
                nc.scalar.activation(ln_sd[:, :], ps[:, 7, 0:SEQ], ACT.Sqrt, bias=ln_eps[:, :]).then_inc(ln_sd_ready, 1)
                eng.wait_ge(normed, l + 1)
                act = v_tok[:, :, :].rearrange("p t n -> p (t n)")
                for c in range(NC):
                    nc.scalar.activation(act[:, SEQ * c:SEQ * (c + 1)], conv_a[:, c, :], ACT.Silu,
                                         bias=params[l][:, LNB + c:LNB + c + 1],
                                         scale=params[l][:, LNG + c:LNG + c + 1]).then_inc(lnsilu_ready, 1)
                eng.wait_ge(lnsilu_ready, NC * (l + 1))
                nc.scalar.activation(branch_hi[0][:, :, :].rearrange("p c n -> p (c n)"), act,
                                     ACT.Copy).then_inc(branch_hi_ready[0], 1)
                hi(Unit(U + U_WO))
                hi(Unit(U + U_WO + 1))
                for t in range(TT):
                    transposed_hi(3 * l + 1, t)
                hi(Unit(U + U_WO + 2))
                hi(Unit(U + U_WO + 3))

            def chunk_silu(done_n, g, nt, width):
                eng.wait_ge(unit_done, done_n)
                if not (isinstance(g, int) and g == 0):
                    eng.wait_ge(g_ready, g)
                for t in range(nt):
                    nc.scalar.activation(silu[:, t, 0:width], ps[:, 4 + t, 0:width], ACT.Silu).then_inc(silu_ready, 1)

            def gT_high(g, nt, width):
                for t in range(nt):
                    eng.wait_ge(gT_done, g + t + 1)
                    k = width // P
                    nc.scalar.activation(gT_hi[:, 0:k, P * t:P * t + P],
                                         ps[:, 4 + t, 0:width].rearrange("p (k n) -> p k n", k=k),
                                         ACT.Copy).then_inc(gT_hi_ready, 1)

            def dense():
                F = MIX_UNITS
                hi(Unit(F + 3))
                chunk_silu(F + 2, 0, TT, BANK)
                for c in range(1, DENSE_CHUNKS):
                    b = F + 6 * c - 2
                    for j in range(4):
                        hi(Unit(b + j))
                    chunk_silu(b + 2, TT * c, TT, BANK)
                    hi(Unit(b + 4))
                    gT_high(TT * (c - 1), TT, BANK)
                    hi(Unit(b + 5))
                b = F + 6 * DENSE_CHUNKS - 2
                hi(Unit(b))
                hi(Unit(b + 1))
                chunk_silu(b + 1, TT * DENSE_CHUNKS, TT, BANK // 2)
                hi(Unit(b + 2))
                gT_high(TT * (DENSE_CHUNKS - 1), TT, BANK)
                hi(Unit(b + 3))
                hi(Unit(b + 4))
                gT_high(TT * DENSE_CHUNKS, TT, BANK // 2)

            norm(0, 0)
            norm(0, 1)
            for l in range(2):
                eng.wait_ge(paramsT_done, l + 1)
                nc.scalar.activation(params[l][:, :], ps[:, l, 0:NPAR], ACT.Copy).then_inc(params_ready, 1)
            for t in range(TT):
                transposed_hi(0, t)
            eng.wait_ge(router_landed, 16)
            nc.scalar.activation(router_hi[:, :, :], router[:, :, :], ACT.Copy).then_inc(router_hi_ready, 1)
            for m in range(3):
                hi(Unit(m))
            mixer(0)
            hi(Unit(MIX_UNITS))
            norm_block(1, 2, MIX_UNITS)
            dense()
            hi(Unit(LAYER_UNITS))
            norm_block(2, 3, LAYER_UNITS)
            mixer(1)
            hi(Unit(MOE0))
            norm_block(3, 5, MOE0)
            eng.wait_ge(shifted_ready, 1)
            nc.scalar.activation(prob[:, :, :], logits[:, :, :], ACT.Exp).then_inc(exp_ready, 1)

            def up(i, c, skip=0):
                units = [moe_unit(kind, i, c, u) for kind in ("w1", "w3") for u in range(2)]
                for u in units[skip:]:
                    hi(u)
                chunk_silu(units[1].n + 1, i * MOE_CHUNKS + (c + GDENSE), 1, BANK)

            def gathered_hi(i):
                for b in range(2):
                    eng.wait_ge(gather_done, i * 2 + b + 1)
                    nc.scalar.activation(actT_hi[:, 4 * b:4 * b + 4, 0:P],
                                         ps[:, 2 + b, :].rearrange("p (k n) -> p k n", k=4),
                                         ACT.Copy).then_inc(hsel_hi_ready, 1)

            def copy_y(i):
                eng.wait_ge(unit_done, moe_unit("down", i, MOE_CHUNKS, 1).n + 1)
                for b in range(2):
                    nc.scalar.activation(y_sb[:, b, :], ps[:, b, :], ACT.Copy).then_inc(y_copied, 1)

            def start(i, prepared):
                gathered_hi(i)
                up(i, 0, prepared)

            def body(i, following):
                def chunk(c):
                    up(i, c)
                    hi(moe_unit("down", i, c, 0))
                    gT_high(i * MOE_CHUNKS + (c + (GDENSE - 1)), 1, BANK)
                    hi(moe_unit("down", i, c, 1))

                chunk(1)
                eng.wait_ge(selT_done, i + 1)
                nc.scalar.activation(selT[:, :], ps[:, 5, 0:SEQ], ACT.Copy).then_inc(selT_ready, 1)
                with eng.Fori(2, MOE_CHUNKS) as c:
                    chunk(c)
                hi(moe_unit("down", i, MOE_CHUNKS, 0))
                gT_high(i * MOE_CHUNKS + (MOE_CHUNKS + GDENSE - 1), 1, BANK)
                if following is None:
                    hi(moe_unit("down", i, MOE_CHUNKS, 1))
                    copy_y(i)
                else:
                    j = following()[0]
                    hi(moe_unit("down", i, MOE_CHUNKS, 1))
                    gathered_hi(j)
                    for u in range(2):
                        hi(moe_unit("w1", j, 0, u))
                    copy_y(i)
                    up(j, 0, 2)

            n = for_items(eng, start, body, 3)
            eng.wait_ge(x_ready, n * 4 + 4 * RESIDUALS)
            for t in range(TT):
                norm(4, t)

        @block.vector
        def _(eng):
            step = [0]

            def done(ins_):
                step[0] += 1
                ins_.then_inc(dve_step, 1)
                eng.wait_ge(dve_step, step[0])

            def lo(u):
                eng.wait_ge(raw_landed[u.raw], u.loads * 16)
                eng.wait_ge(unit_hi, u.n + 1)
                nc.vector.tensor_tensor(w_lo[u.split][:, :], raw[u.raw][:, :], w_hi[u.split][:, :],
                                        ALU.subtract).then_inc(unit_lo, 1)

            def norm(k, t):
                s = 2 * k + t
                eng.wait_ge(sumsq_ready, s + 1)
                a, y, w = (m[:, s:s + 1] for m in (sumsq, rstd, newton))
                done(nc.vector.tensor_scalar(a, a, RMS_EPS, None, ALU.add))
                done(nc.vector.tensor_scalar(y.bitcast(I32), a.bitcast(I32), -0.5, float(0x5F3759DF),
                                             ALU.mult, ALU.add))
                for _ in range(3):
                    done(nc.vector.scalar_tensor_tensor(out=w, in0=y, scalar=a, in1=y, op0=ALU.mult, op1=ALU.mult))
                    done(nc.vector.tensor_scalar(w, w, -0.5, 1.5, ALU.mult, ALU.add))
                    done(nc.vector.tensor_tensor(y, y, w, ALU.mult))
                eng.wait_ge(gain_landed, 16 * (k + 1))
                nc.vector.scalar_tensor_tensor(out=h[:, t, :], in0=x[:, t, :], scalar=rstd[:, s:s + 1],
                                               in1=gain[:, :], op0=ALU.mult, op1=ALU.mult).then_inc(h_ready, 1)

            def residual(q, t, end):
                if t == 0:
                    eng.wait_ge(res_tile0_done, q + 1)
                else:
                    eng.wait_ge(unit_done, end)
                for b in range(2):
                    part = x[:, t, BANK * b:BANK * (b + 1)]
                    nc.vector.tensor_tensor(part, part, ps[:, 2 * t + b, :], ALU.add).then_inc(x_ready, 1)

            def transposed_lo(r, t):
                for b in range(2):
                    eng.wait_ge(tT_hi, 4 * r + 2 * t + b + 1)
                    part = slice(4 * b, 4 * b + 4), slice(P * t, P * t + P)
                    nc.vector.tensor_tensor(actT_lo[:, part[0], part[1]],
                                            ps[:, 4 + 2 * t + b, :].rearrange("p (k n) -> p k n", k=4),
                                            actT_hi[:, part[0], part[1]], ALU.subtract).then_inc(tT_lo, 1)

            def norm_block(k, r, m):
                for t in range(TT):
                    residual(k - 1, t, m)
                for t in range(TT):
                    norm(k, t)
                lo(Unit(m + 1))
                for t in range(TT):
                    transposed_lo(r, t)
                lo(Unit(m + 2))

            def mixer(l):
                U = LAYER_UNITS * l
                par = params[l]

                def product(k, dst, tmp, tmp_ready, ready):
                    eng.wait_ge(unit_done, U + 2 * k + 2)
                    for t in range(TT):
                        eng.wait_ge(tmp_ready, TT * l + t + 1)
                        nc.vector.tensor_tensor(dst[:, t, :], ps[:, 2 * (k % 3) + t, :], tmp[:, t, :],
                                                ALU.mult).then_inc(ready, 1)

                taps = [(k, c) for k in range(KA) for c in range(NC - 1)]
                mine = []

                def conv_taps(n):
                    for _ in range(min(n, len(taps))):
                        k, c = taps.pop(0)
                        if not mine:
                            eng.wait_ge(convin_a_ready, TT * (l + 1))
                            eng.wait_ge(params_ready, 2)
                        if k:
                            eng.wait_ge(conv_a_dve, len(taps_all) * l + len(mine) - (NC - 2))
                        src = convin_a[:, c, k:k + SEQ]
                        w = par[:, k * NC + c:k * NC + c + 1]
                        if k == 0:
                            ins_ = nc.vector.tensor_scalar(conv_a[:, c, :], src, w, par[:, BIAS + c:BIAS + c + 1],
                                                           ALU.mult, ALU.add)
                        else:
                            ins_ = nc.vector.scalar_tensor_tensor(out=conv_a[:, c, :], in0=src, scalar=w,
                                                                  in1=conv_a[:, c, :], op0=ALU.mult, op1=ALU.add)
                        ins_.then_inc(conv_a_dve, 1)
                        mine.append((k, c))

                taps_all = list(taps)
                for j in range(3, 6):
                    lo(Unit(U + j))
                product(A_VAL, a_tok, gates[:, :, BANK:2 * BANK], sig_ready, a_ready)
                for j in range(6, 9):
                    lo(Unit(U + j))
                conv_taps(8)
                lo(Unit(U + 9))
                product(S_X, v_tok, gates[:, :, 0:BANK], c_ready, v_ready)
                conv_taps(6)
                for j in range(10, U_WB):
                    lo(Unit(U + j))
                    conv_taps(10)
                conv_taps(len(taps))
                eng.wait_ge(conv_b_pool, l + 1)
                for t in range(TT):
                    eng.wait_ge(bT_done, TT * l + t + 1)
                    part = conv_b[:, :, P * t:P * t + P]
                    nc.vector.tensor_tensor(part, part, ps[:, 6 + t, :].rearrange("p (c n) -> p c n", c=NC),
                                            ALU.mult).then_inc(ub_ready, 1)
                lo(Unit(U + U_WB))
                eng.wait_ge(ub_ready, TT * (l + 1))
                eng.wait_ge(branch_hi_ready[1], l + 1)
                nc.vector.tensor_tensor(branch_lo[1][:, :, :], conv_b[:, :, :], branch_hi[1][:, :, :],
                                        ALU.subtract).then_inc(branch_lo_ready[1], 1)
                eng.wait_ge(mean_done, l + 1)
                nc.vector.tensor_tensor(conv_a[:, :, :], conv_a[:, :, :],
                                        ps[:, 6:7, 0:SEQ].to_broadcast([P, NC, SEQ]),
                                        ALU.subtract).then_inc(centred, 1)
                lo(Unit(U + U_WB + 1))
                eng.wait_ge(ln_sd_ready, l + 1)
                done(nc.vector.reciprocal(ln_rstd[:, :], ln_sd[:, :]))
                eng.wait_ge(centred, l + 1)
                nc.vector.tensor_tensor(conv_a[:, :, :], conv_a[:, :, :],
                                        ln_rstd[:, :].rearrange("p (a n) -> p a n", a=1).to_broadcast([P, NC, SEQ]),
                                        ALU.mult).then_inc(normed, 1)
                lo(Unit(U + U_WA))
                lo(Unit(U + U_WA + 1))
                eng.wait_ge(branch_hi_ready[0], l + 1)
                nc.vector.tensor_tensor(branch_lo[0][:, :, :].rearrange("p c n -> p (c n)"),
                                        v_tok[:, :, :].rearrange("p t n -> p (t n)"),
                                        branch_hi[0][:, :, :].rearrange("p c n -> p (c n)"),
                                        ALU.subtract).then_inc(branch_lo_ready[0], 1)
                eng.wait_ge(unit_done, U + U_WA)
                eng.wait_ge(gate_ready, 4 * (l + 1))
                for t in range(TT):
                    for b in range(2):
                        done(nc.vector.tensor_tensor(h[:, t, BANK * b:BANK * (b + 1)], ps[:, 2 * t + b, :],
                                                     gates[:, t, D + BANK * b:D + BANK * (b + 1)], ALU.mult))
                lo(Unit(U + U_WO))
                for t in range(TT):
                    if t == 0:
                        eng.wait_ge(ya_tile0_done, l + 1)
                    else:
                        eng.wait_ge(unit_done, U + U_WO)
                    for b in range(2):
                        ga = gates[:, t, BANK * b:BANK * (b + 1)]
                        done(nc.vector.tensor_tensor(ga, ps[:, 4 + 2 * t + b, :], ga, ALU.mult))
                    nc.vector.tensor_tensor(h[:, t, :], h[:, t, :], gates[:, t, 0:D], ALU.add).then_inc(merged_ready, 1)
                lo(Unit(U + U_WO + 1))
                for t in range(TT):
                    transposed_lo(3 * l + 1, t)
                lo(Unit(U + U_WO + 2))
                lo(Unit(U + U_WO + 3))

            def chunk_g(done_n, g, nt, width):
                eng.wait_ge(unit_done, done_n)
                for t in range(nt):
                    eng.wait_ge(silu_ready, g + t + 1)
                    nc.vector.tensor_tensor(g_tok[:, t, 0:width], ps[:, 6 + t, 0:width], silu[:, t, 0:width],
                                            ALU.mult).then_inc(g_ready, 1)

            def gT_low(g, nt, width):
                k = width // P
                for t in range(nt):
                    eng.wait_ge(gT_hi_ready, g + t + 1)
                    nc.vector.tensor_tensor(gT_lo[:, 0:k, P * t:P * t + P],
                                            ps[:, 4 + t, 0:width].rearrange("p (k n) -> p k n", k=k),
                                            gT_hi[:, 0:k, P * t:P * t + P], ALU.subtract).then_inc(gT_lo_ready, 1)

            def dense():
                F = MIX_UNITS
                lo(Unit(F + 3))
                chunk_g(F + 4, 0, TT, BANK)
                for c in range(1, DENSE_CHUNKS):
                    b = F + 6 * c - 2
                    for j in range(5):
                        lo(Unit(b + j))
                    gT_low(TT * (c - 1), TT, BANK)
                    lo(Unit(b + 5))
                    chunk_g(b + 4, TT * c, TT, BANK)
                b = F + 6 * DENSE_CHUNKS - 2
                for j in range(3):
                    lo(Unit(b + j))
                gT_low(TT * (DENSE_CHUNKS - 1), TT, BANK)
                lo(Unit(b + 3))
                chunk_g(b + 2, TT * DENSE_CHUNKS, TT, BANK // 2)
                lo(Unit(b + 4))
                gT_low(TT * DENSE_CHUNKS, TT, BANK // 2)

            def routing():
                v = nc.vector
                eng.wait_ge(logits_done, TT)
                done(v.tensor_copy(logits[:, :, :], ps[:, 4, 0:TT * E].rearrange("p (t e) -> p t e", t=TT)))
                one = logits[:, :, :].rearrange("p t (e a) -> p t e a", a=1).to_broadcast([P, TT, E, E])
                other = logits[:, :, :].rearrange("p t (a j) -> p t a j", a=1).to_broadcast([P, TT, E, E])
                for t in range(TT):
                    done(v.tensor_tensor(pair_gt[:, t], other[:, t], one[:, t], ALU.is_gt))
                    done(v.tensor_tensor(pair_eq[:, t], other[:, t], one[:, t], ALU.is_equal))
                    done(v.tensor_tensor(pair_eq[:, t], pair_eq[:, t], earlier[:, :, :], ALU.mult))
                    done(v.tensor_tensor(pair_gt[:, t], pair_gt[:, t], pair_eq[:, t], ALU.add))
                    done(v.tensor_reduce(rank[:, t, :], pair_gt[:, t], AX.X, ALU.add))
                v.tensor_scalar(chosen[:, :, :], rank[:, :, :], 1.5, None, ALU.is_lt).then_inc(chosen_ready, 1)
                done(v.tensor_reduce(top[:, :], logits[:, :, :], AX.X, ALU.max))
                v.tensor_tensor(logits[:, :, :], logits[:, :, :],
                                top[:, :].rearrange("p (t a) -> p t a", a=1).to_broadcast([P, TT, E]),
                                ALU.subtract).then_inc(shifted_ready, 1)
                eng.wait_ge(chosen_ready, 1)
                eng.wait_ge(exp_ready, 1)
                done(v.tensor_tensor(prob[:, :, :], prob[:, :, :], chosen[:, :, :], ALU.mult))
                done(v.tensor_reduce(total[:, :], prob[:, :, :], AX.X, ALU.add))
                done(v.reciprocal(total[:, :], total[:, :]))
                done(v.tensor_tensor(route[:, :, TT:2 * TT].rearrange("p e t -> p t e"), prob[:, :, :],
                                     total[:, :].rearrange("p (t a) -> p t a", a=1).to_broadcast([P, TT, E]), ALU.mult))
                eng.wait_ge(count_done, 1)
                counts = ps[:, 5, :]
                done(v.scalar_tensor_tensor(out=place[:, :, :], in0=counts[:, 0:TT * E].rearrange("p (t e) -> p t e", t=TT),
                                            scalar=1.0, in1=chosen[:, :, :], op0=ALU.add, op1=ALU.mult))
                done(v.tensor_scalar(route[:, :, 0:TT].rearrange("p e t -> p t e"), place[:, :, :], -1.0, None, ALU.add))
                done(v.tensor_scalar(over[:, :], counts[:, TT * E:TT * E + E], float(P) + 0.5, None, ALU.is_gt))
                over_j = over[:, :].rearrange("p (a j) -> p a j", a=1).to_broadcast([P, E, E])
                done(v.tensor_tensor(over_pairs[:, :, :], over_j, earlier[:, :, :], ALU.mult))
                done(v.tensor_reduce(over_before[:, :], over_pairs[:, :, :], AX.X, ALU.add))
                done(v.tensor_tensor(over_index[:, :], over[:, :], iota_e[:, :], ALU.mult))
                done(v.tensor_tensor(over_pairs[:, :, :],
                                     iota_e[:, :].rearrange("p (e a) -> p e a", a=1).to_broadcast([P, E, E]),
                                     over_before[:, :].rearrange("p (a j) -> p a j", a=1).to_broadcast([P, E, E]),
                                     ALU.is_equal))
                done(v.tensor_tensor(over_pairs[:, :, :], over_pairs[:, :, :],
                                     over_index[:, :].rearrange("p (a j) -> p a j", a=1).to_broadcast([P, E, E]), ALU.mult))
                done(v.tensor_reduce(items_f[:, 1 + E:1 + 2 * E], over_pairs[:, :, :], AX.X, ALU.add))
                done(v.tensor_copy(items_f[:, 1:1 + E], iota_e[:, :]))
                done(v.tensor_reduce(items_f[:, 0:1], over[:, :], AX.X, ALU.add))
                done(v.tensor_scalar(items_f[:, 0:1], items_f[:, 0:1], float(E), None, ALU.add))
                v.tensor_copy(items[:, :], items_f[:, :]).then_inc(items_ready, 1)

            def select(i, e, group, read_by=None):
                if i is not e:
                    e = eng.value_load(items[0:1, bass.ds(i + 1, 1)], min_val=0, max_val=E - 1)
                if read_by is not None:
                    eng.wait_ge(cur_ready, read_by * 2 + 2)
                nc.vector.tensor_copy(cur[:, :].rearrange("p (a n) -> p a n", a=1),
                                      route[:, bass.ds(e, 1), :]).then_inc(cur_ready, 1)
                eng.wait_ge(cur_ready, i * 2 + 1)
                if read_by is not None:
                    eng.wait_ge(selT_done, read_by + 1)
                for t in range(TT):
                    nc.vector.tensor_scalar(sel[:, t, :], iota_s[:, P * group:P * group + P], cur[:, t:t + 1], None,
                                            ALU.is_equal).then_inc(sel_ready, 1)

            def gathered_lo(i):
                for b in range(2):
                    eng.wait_ge(hsel_hi_ready, i * 2 + b + 1)
                    nc.vector.tensor_tensor(actT_lo[:, 4 * b:4 * b + 4, 0:P],
                                            ps[:, 2 + b, :].rearrange("p (k n) -> p k n", k=4),
                                            actT_hi[:, 4 * b:4 * b + 4, 0:P], ALU.subtract).then_inc(hsel_lo_ready, 1)

            def add_back(i, t):
                eng.wait_ge(cur_ready, i * 2 + 2)
                for b in range(2):
                    eng.wait_ge(scatter_done, i * 4 + 2 * t + b + 1)
                    part = x[:, t, BANK * b:BANK * (b + 1)]
                    nc.vector.scalar_tensor_tensor(out=part, in0=ps[:, scatter_banks[t][b], :],
                                                   scalar=cur_weight[:, t:t + 1], in1=part,
                                                   op0=ALU.mult, op1=ALU.add).then_inc(x_ready, 1)

            def up(i, c, skip=0, last=4):
                units = [moe_unit(kind, i, c, u) for kind in ("w1", "w3") for u in range(2)]
                for u in units[skip:last]:
                    lo(u)
                return units[3].n + 1

            def start(i, prepared):
                select(i, i if isinstance(i, int) else None, 0 if isinstance(i, int) else 1)
                gathered_lo(i)
                first_g(i, up(i, 0, prepared))

            def first_g(i, n):
                for u in range(2):
                    lo(moe_unit("w1", i, 1, u))
                chunk_g(n, i * MOE_CHUNKS + GDENSE, 1, BANK)

            def body(i, following):
                def chunk(c, ahead=0):
                    n = up(i, c, ahead)
                    lo(moe_unit("down", i, c, 0))
                    gT_low(i * MOE_CHUNKS + (c + (GDENSE - 1)), 1, BANK)
                    lo(moe_unit("down", i, c, 1))
                    chunk_g(n, i * MOE_CHUNKS + (c + GDENSE), 1, BANK)

                chunk(1, 2)
                eng.wait_ge(x_ready, i * 4 + 4 * RESIDUALS)
                nc.vector.tensor_copy(cur_weight[:, :], cur[:, TT:2 * TT]).then_inc(cur_ready, 1)
                if following is not None:
                    select(*following(), read_by=i)
                with eng.Fori(2, MOE_CHUNKS) as c:
                    chunk(c)
                lo(moe_unit("down", i, MOE_CHUNKS, 0))
                gT_low(i * MOE_CHUNKS + (MOE_CHUNKS + GDENSE - 1), 1, BANK)
                if following is None:
                    lo(moe_unit("down", i, MOE_CHUNKS, 1))
                    for t in range(TT):
                        add_back(i, t)
                else:
                    j = following()[0]
                    lo(moe_unit("down", i, MOE_CHUNKS, 1))
                    gathered_lo(j)
                    up(j, 0, 0, 3)
                    add_back(i, 0)
                    n = up(j, 0, 3)
                    add_back(i, 1)
                    first_g(j, n)

            for t in range(TT):
                norm(0, t)
            for t in range(TT):
                transposed_lo(0, t)
            eng.wait_ge(router_landed, 16)
            eng.wait_ge(router_hi_ready, 1)
            nc.vector.tensor_tensor(router_lo[:, :, :], router[:, :, :], router_hi[:, :, :],
                                    ALU.subtract).then_inc(router_ready, 1)
            for m in range(3):
                lo(Unit(m))
            mixer(0)
            lo(Unit(MIX_UNITS))
            norm_block(1, 2, MIX_UNITS)
            dense()
            lo(Unit(LAYER_UNITS))
            norm_block(2, 3, LAYER_UNITS)
            mixer(1)
            lo(Unit(MOE0))
            norm_block(3, 5, MOE0)
            routing()
            for_items(eng, start, body, 3)
            for t in range(TT):
                norm(4, t)

        @block.tensor
        def _(eng):
            mm = nc.tensor.matmul

            def product(dst, act, w, start, stop):
                (act_hi, act_lo), (wh, wl) = act, w
                mm(dst, act_hi, wh, start=start, stop=False)
                mm(dst, act_hi, wl, start=False, stop=False)
                return mm(dst, act_lo, wh, start=False, stop=stop)

            def weights(u, a, b):
                return w_hi[u.split][:, a:b], w_lo[u.split][:, a:b]

            def stationary(pair, k, t):
                return tuple(m[:, k, P * t:P * t + P] for m in pair)

            act = (actT_hi, actT_lo)
            gT = (gT_hi, gT_lo)

            def up_unit(u, j, bank, nt, width=BANK):
                eng.wait_ge(unit_lo, u.n + 1)
                k = UNIT // width
                for q in range(k):
                    for t in range(nt):
                        last = product(ps[:, bank + t, 0:width], stationary(act, k * j + q, t),
                                       weights(u, width * q, width * (q + 1)),
                                       start=(j == 0 and q == 0), stop=(k * j + q == KD - 1))
                last.then_inc(unit_done, 1)

            def transposes(r, t, ready, value):
                eng.wait_ge(ready, value)
                for k in range(KD):
                    last = nc.tensor.transpose(ps[:, 4 + 2 * t + k // 4, P * (k % 4):P * (k % 4) + P],
                                               h[:, t, P * k:P * k + P], ident[:, :])
                last.then_inc(tT_done, 1)

            def channel_transposes(src, l, ready, done_sem):
                for t in range(TT):
                    eng.wait_ge(ready, TT * l + t + 1)
                    for c in range(NC):
                        last = nc.tensor.transpose(ps[:, 6 + t, P * c:P * c + P], src[:, t, P * c:P * c + P], ident[:, :])
                    last.then_inc(done_sem, 1)

            def mixer(l):
                U = LAYER_UNITS * l

                def z(k):
                    for j in range(2):
                        up_unit(Unit(U + 2 * k + j), j, 2 * (k % 3), TT)

                eng.wait_ge(tT_lo, 4 * 3 * l + 4)
                z(A_VAL)
                z(A_GATE)
                z(S_C)
                channel_transposes(a_tok, l, a_ready, aT_done)
                z(S_X)
                z(S_B)
                eng.wait_ge(convin_a_ready, TT * (l + 1))
                channel_transposes(v_tok, l, v_ready, vT_done)
                z(G0)
                eng.wait_ge(convin_b_ready, TT * (l + 1))
                channel_transposes(b_tok, l, b_ready, bT_done)
                z(G0 + 1)
                z(G0 + 2)
                eng.wait_ge(gate_ready, 4 * l + 1)
                z(G0 + 3)
                eng.wait_ge(conv_a_dve, (NC - 1) * KA * (l + 1))
                eng.wait_ge(conv_a_pool, l + 1)
                eng.wait_ge(ub_ready, TT * (l + 1))
                for c in range(NC):
                    last = mm(ps[:, 6, 0:SEQ], mean_of[:, :], conv_a[:, c, :], start=(c == 0), stop=(c == NC - 1))
                last.then_inc(mean_done, 1)
                branch = [(branch_hi[b], branch_lo[b]) for b in range(2)]
                eng.wait_ge(gate_ready, 4 * l + 3)
                eng.wait_ge(branch_lo_ready[1], l + 1)
                for j in range(2):
                    u = Unit(U + U_WB + j)
                    eng.wait_ge(unit_lo, u.n + 1)
                    for q in range(2):
                        for t in range(TT):
                            for b in range(2):
                                last = product(ps[:, 2 * t + b, :], stationary(branch[1], 2 * j + q, t),
                                               weights(u, D * q + BANK * b, D * q + BANK * (b + 1)),
                                               start=(j == 0 and q == 0), stop=(j == 1 and q == 1))
                    last.then_inc(unit_done, 1)
                    if j == 0:
                        eng.wait_ge(squares_ready, l + 1)
                        for c in range(NC):
                            last = mm(ps[:, 7, 0:SEQ], mean_of[:, :],
                                      a_tok[:, :, :].rearrange("p t n -> p (t n)")[:, SEQ * c:SEQ * (c + 1)],
                                      start=(c == 0), stop=(c == NC - 1))
                        last.then_inc(var_done, 1)
                eng.wait_ge(gate_ready, 4 * l + 4)
                eng.wait_ge(normed, l + 1)
                eng.wait_ge(branch_lo_ready[0], l + 1)
                down_by_tile(U + U_WA, 2, branch[0], 0, 4, True, True, ya_tile0_done)
                for t in range(TT):
                    transposes(3 * l + 1, t, merged_ready, TT * l + t + 1)
                eng.wait_ge(tT_lo, 4 * (3 * l + 1) + 4)
                down_by_tile(U + U_WO, 2, act, 0, 0, True, False)
                down_by_tile(U + U_WO + 2, 2, act, 4, 0, False, True, res_tile0_done)

            def down_by_tile(n, count, left, k0, bank, first, final, tile0_done=None):
                units = [Unit(n + j) for j in range(count)]
                for u in units:
                    eng.wait_ge(unit_lo, u.n + 1)
                for t in range(TT):
                    for j, u in enumerate(units):
                        for q in range(2):
                            for b in range(2):
                                k = 2 * j + q
                                last = product(ps[:, bank + 2 * t + b, :], stationary(left, k0 + k, t),
                                               weights(u, D * q + BANK * b, D * q + BANK * (b + 1)),
                                               start=first and k == 0, stop=final and k == 2 * count - 1)
                        if t == TT - 1:
                            last.then_inc(unit_done, 1)
                    if t == 0 and tile0_done is not None:
                        last.then_inc(tile0_done, 1)

            def g_transposes(g, nt, width, silu_count):
                if silu_count is not None:
                    eng.wait_ge(silu_ready, silu_count)
                for t in range(nt):
                    eng.wait_ge(g_ready, g + t + 1)
                    for k in range(width // P):
                        last = nc.tensor.transpose(ps[:, 4 + t, P * k:P * k + P], g_tok[:, t, P * k:P * k + P], ident[:, :])
                    last.then_inc(gT_done, 1)

            def dense():
                F = MIX_UNITS
                eng.wait_ge(tT_lo, 4 * 2 + 4)
                for j in range(2):
                    up_unit(Unit(F + j), j, 4, TT)
                for j in range(2):
                    up_unit(Unit(F + 2 + j), j, 6, TT)
                for c in range(1, DENSE_CHUNKS):
                    b = F + 6 * c - 2
                    for j in range(2):
                        up_unit(Unit(b + j), j, 4, TT)
                    eng.wait_ge(g_ready, TT * c)
                    up_unit(Unit(b + 2), 0, 6, TT)
                    g_transposes(TT * (c - 1), TT, BANK, TT * (c + 1))
                    up_unit(Unit(b + 3), 1, 6, TT)
                    eng.wait_ge(gT_lo_ready, TT * c)
                    dense_down(b + 4, c == 1, False)
                b = F + 6 * DENSE_CHUNKS - 2
                up_unit(Unit(b), 0, 4, TT, BANK // 2)
                eng.wait_ge(g_ready, TT * DENSE_CHUNKS)
                up_unit(Unit(b + 1), 0, 6, TT, BANK // 2)
                g_transposes(TT * (DENSE_CHUNKS - 1), TT, BANK, TT * (DENSE_CHUNKS + 1))
                eng.wait_ge(gT_lo_ready, TT * DENSE_CHUNKS)
                dense_down(b + 2, False, False)
                g_transposes(TT * DENSE_CHUNKS, TT, BANK // 2, None)
                eng.wait_ge(gT_lo_ready, TT * (DENSE_CHUNKS + 1))
                down_by_tile(b + 4, 1, gT, 0, 0, False, True, res_tile0_done)

            def dense_down(n, first, final):
                for j in range(2):
                    u = Unit(n + j)
                    eng.wait_ge(unit_lo, u.n + 1)
                    for q in range(2):
                        for t in range(TT):
                            for b in range(2):
                                last = product(ps[:, 2 * t + b, :], stationary(gT, 2 * j + q, t),
                                               weights(u, D * q + BANK * b, D * q + BANK * (b + 1)),
                                               start=first and j == 0 and q == 0, stop=final)
                    last.then_inc(unit_done, 1)

            def routing():
                eng.wait_ge(tT_lo, 4 * 5 + 4)
                eng.wait_ge(router_ready, 1)
                for t in range(TT):
                    for k in range(KD):
                        for a, left in enumerate((actT_hi, actT_lo)):
                            for b, right in enumerate((router_hi, router_lo)):
                                last = mm(ps[:, 4, E * t:E * t + E], left[:, k, P * t:P * t + P], right[:, k, :],
                                          start=(k == a == b == 0), stop=(k == KD - 1 and a == b == 1))
                    last.then_inc(logits_done, 1)
                eng.wait_ge(chosen_ready, 1)
                counts = ps[:, 5, :]
                mm(counts[:, 0:E], before[:, :], chosen[:, 0, :], start=True, stop=True)
                mm(counts[:, E:2 * E], ones[:, :], chosen[:, 0, :], start=True, stop=False)
                mm(counts[:, E:2 * E], before[:, :], chosen[:, 1, :], start=False, stop=True)
                mm(counts[:, 2 * E:3 * E], ones[:, :], chosen[:, 0, :], start=True, stop=False)
                mm(counts[:, 2 * E:3 * E], ones[:, :], chosen[:, 1, :], start=False, stop=True).then_inc(count_done, 1)

            def gather(i, b):
                if b == 0:
                    eng.wait_ge(sel_ready, i * TT + TT)
                for k in range(4 * b, 4 * b + 4):
                    for t in range(TT):
                        last = mm(ps[:, 2 + b, P * (k % 4):P * (k % 4) + P], h[:, t, P * k:P * k + P], sel[:, t, :],
                                  start=(t == 0), stop=(t == TT - 1))
                last.then_inc(gather_done, 1)

            def g_of(i, c):
                return i * MOE_CHUNKS + (c + GDENSE)

            def down(i, c, first, final=False):
                eng.wait_ge(gT_lo_ready, g_of(i, c))
                for j in range(2):
                    u = moe_unit("down", i, c, j)
                    eng.wait_ge(unit_lo, u.n + 1)
                    for q in range(2):
                        for b in range(2):
                            last = product(ps[:, b, :], stationary(gT, 2 * j + q, 0),
                                           weights(u, D * q + BANK * b, D * q + BANK * (b + 1)),
                                           start=first and j == 0 and q == 0,
                                           stop=final and j == 1 and q == 1)
                    last.then_inc(unit_done, 1)

            def up_w1(i, c):
                for j in range(2):
                    up_unit(moe_unit("w1", i, c, j), j, 4, 1)

            def up_w3(i, c):
                eng.wait_ge(g_ready, g_of(i, c))
                up_unit(moe_unit("w3", i, c, 0), 0, 6, 1)
                if not isinstance(c, int) or c:
                    g_transposes(g_of(i, c) - 1, 1, BANK, g_of(i, c) + 1)
                up_unit(moe_unit("w3", i, c, 1), 1, 6, 1)

            def scatter(i):
                eng.wait_ge(selT_ready, i + 1)
                for t in range(TT):
                    for b in range(2):
                        if t == 0:
                            eng.wait_ge(y_copied, i * 2 + b + 1)
                        mm(ps[:, scatter_banks[t][b], :], selT[:, P * t:P * t + P], y_sb[:, b, :],
                           start=True, stop=True).then_inc(scatter_done, 1)

            def start(i, prepared):
                gather(i, 0)
                gather(i, 1)
                eng.wait_ge(hsel_lo_ready, i * 2 + 2)
                up_w1(i, 0)
                up_w3(i, 0)

            def body(i, following):
                up_w1(i, 1)
                up_w3(i, 1)
                eng.wait_ge(x_ready, i * 4 + 4 * RESIDUALS)
                for t in range(TT):
                    last = nc.tensor.transpose(ps[:, 5, P * t:P * t + P], sel[:, t, :], ident[:, :])
                last.then_inc(selT_done, 1)
                down(i, 1, True)
                with eng.Fori(2, MOE_CHUNKS) as c:
                    up_w1(i, c)
                    up_w3(i, c)
                    down(i, c, False)
                if following is None:
                    g_transposes(g_of(i, MOE_CHUNKS - 1), 1, BANK, None)
                    down(i, MOE_CHUNKS, False, True)
                    scatter(i)
                else:
                    j = following()[0]
                    g_transposes(g_of(i, MOE_CHUNKS - 1), 1, BANK, None)
                    gather(j, 0)
                    gather(j, 1)
                    down(i, MOE_CHUNKS, False, True)
                    eng.wait_ge(hsel_lo_ready, j * 2 + 2)
                    up_w1(j, 0)
                    scatter(i)
                    up_w3(j, 0)

            eng.wait_ge(pool_step, 2)
            eng.wait_ge(consts_ready, 3)
            eng.wait_ge(params_landed, 16 * 10)
            for l in range(2):
                a, b = params_in[l]
                nb = NPAR - KA * NC
                nc.tensor.transpose(ps[:, l, 0:KA * NC], a[0:KA * NC, :], ident[0:KA * NC, 0:KA * NC])
                nc.tensor.transpose(ps[:, l, KA * NC:NPAR], b[0:nb, :], ident[0:nb, 0:nb]).then_inc(paramsT_done, 1)
            for t in range(TT):
                transposes(0, t, h_ready, t + 1)
            eng.wait_ge(params_ready, 2)
            mixer(0)
            for t in range(TT):
                transposes(2, t, h_ready, 2 + t + 1)
            dense()
            for t in range(TT):
                transposes(3, t, h_ready, 4 + t + 1)
            mixer(1)
            for t in range(TT):
                transposes(5, t, h_ready, 6 + t + 1)
            routing()
            for_items(eng, start, body, 3)


def kernel(**inputs):
    import numpy as np
    from concourse import bacc
    from concourse.bass_utils import run_bass_kernel_spmd

    nc = bacc.Bacc("TRN2", target_bir_lowering=False, num_devices=1)
    arrays, ins = {}, {}
    for name, value in inputs.items():
        a = np.ascontiguousarray(value)
        arrays[f"in_{name}"] = a
        ins[name] = nc.dram_tensor(f"in_{name}", a.shape, mybir.dt.from_np(a.dtype), kind="ExternalInput").ap()
    out = nc.dram_tensor("out", inputs["x"].shape, F32, kind="ExternalOutput").ap()
    trunk(nc, ins, out)
    result = run_bass_kernel_spmd(nc, [arrays], core_ids=[0])
    return result.results[0]["out"]
```

```python
from contextlib import ExitStack

import concourse.bass as bass
from concourse import mybir

F32 = mybir.dt.float32
F32R = mybir.dt.float32r
I32 = mybir.dt.int32
ALU = mybir.AluOpType
ACT = mybir.ActivationFunctionType
AX = mybir.AxisListType

P = 128
BANK = 512
UNIT = 2048
RAW_SLOTS = 6
SPLIT_SLOTS = 3
RMS_EPS = 1e-6
LN_EPS = 1e-5


class Unit:

    def __init__(self, fixed, item=0, step=0):
        self.n = item * 42 + step * 6 + fixed
        self.first_round = fixed < SPLIT_SLOTS
        self.first_raw_round = fixed < RAW_SLOTS
        self.raw = fixed % RAW_SLOTS
        self.split = fixed % SPLIT_SLOTS
        self.loads = item * 7 + step + (fixed // RAW_SLOTS + 1)


def trunk(nc, ins, out):
    x_in = ins["x"]
    _, SEQ, D = x_in.shape
    TT = SEQ // P
    KD = D // P
    KA, C = ins["l0_conv_a"].shape
    KB, CS = ins["l0_conv_b"].shape
    NC = C // P
    FD = ins["l0_ffn_w1"].shape[1]
    E, _, FE = ins["l1_moe_w1"].shape
    assert TT == 2 and KD == 8 and NC == 4 and CS == C == BANK and D == 2 * BANK
    MOE_CHUNKS = FE // BANK
    assert MOE_CHUNKS == 7 and FE % BANK == 0
    DENSE_CHUNKS = FD // BANK
    assert FD == DENSE_CHUNKS * BANK + BANK // 2

    A_VAL, A_GATE, S_C, S_X, S_B, G0 = range(6)
    z_cols = [0, C, 2 * C + CS, 2 * C + 2 * CS, 2 * C] + [2 * C + 3 * CS + BANK * j for j in range(4)]
    NZ = len(z_cols)
    U_WB = 2 * NZ
    U_WA = U_WB + 2
    U_WO = U_WA + 2
    MIX_UNITS = U_WO + 4
    FFN_UNITS = 6 * DENSE_CHUNKS + 3
    LAYER_UNITS = MIX_UNITS + FFN_UNITS
    MOE0 = LAYER_UNITS + MIX_UNITS
    BIAS, LNG, LNB, CONVB = (KA * NC + NC * j for j in range(4))
    NPAR = CONVB + KB * NC
    GDENSE = TT * (DENSE_CHUNKS + 1)

    def rows(w, k):
        return w.rearrange("(k p) n -> p k n", p=P)[:, k[0]:k[1], :]

    def layer_units(l):
        w_in = ins[f"l{l}_w_in"]
        out_ = [rows(w_in, (4 * u, 4 * u + 4))[:, :, c:c + BANK] for c in z_cols for u in range(2)]
        for name, tiles in (("w_b", NC), ("w_a", NC), ("w_o", KD)):
            out_ += [rows(ins[f"l{l}_{name}"], (j, j + 2)) for j in range(0, tiles, 2)]
        return out_

    def dense_units():
        w1, w3, w2 = (ins[f"l0_ffn_{n}"] for n in ("w1", "w3", "w2"))
        out_ = []
        for c in range(DENSE_CHUNKS):
            for w in (w1, w3):
                out_ += [rows(w, (4 * u, 4 * u + 4))[:, :, BANK * c:BANK * (c + 1)] for u in range(2)]
            if c:
                out_ += [rows(w2, (4 * (c - 1) + 2 * u, 4 * (c - 1) + 2 * u + 2)) for u in range(2)]
        last = BANK * DENSE_CHUNKS
        out_ += [rows(w, (0, KD))[:, :, last:FD] for w in (w1, w3)]
        out_ += [rows(w2, (4 * DENSE_CHUNKS - 4 + 2 * u, 4 * DENSE_CHUNKS - 2 + 2 * u)) for u in range(2)]
        out_ += [rows(w2, (4 * DENSE_CHUNKS, FD // P))]
        return out_

    static_units = layer_units(0) + dense_units() + layer_units(1)
    assert len(static_units) == MOE0
    moe_up = [ins[f"l1_moe_{n}"].rearrange("e (k p) f -> e p k f", p=P) for n in ("w1", "w3")]
    moe_down = ins["l1_moe_w2"].rearrange("e (k p) n -> e p k n", p=P)

    with ExitStack() as ctx:
        def sb(name, shape, dt=F32):
            return ctx.enter_context(nc.sbuf_tensor(name, [P] + shape, dt))

        def sem(name):
            return ctx.enter_context(nc.semaphore(name))

        raw = [sb(f"raw{s}", [UNIT]) for s in range(RAW_SLOTS)]
        w_hi = [sb(f"w_hi{s}", [UNIT], F32R) for s in range(SPLIT_SLOTS)]
        w_lo = [sb(f"w_lo{s}", [UNIT], F32R) for s in range(SPLIT_SLOTS)]
        x = sb("x", [TT, D])
        h = sb("h", [TT, D])
        gates = sb("gates", [TT, 2 * D])
        a_tok = sb("a_tok", [TT, BANK])
        v_tok = sb("v_tok", [TT, BANK])
        b_tok = sb("b_tok", [TT, BANK])
        actT_hi = sb("actT_hi", [KD, SEQ], F32R)
        actT_lo = sb("actT_lo", [KD, SEQ], F32R)
        branch_hi = [sb(f"branch_hi{b}", [NC, SEQ], F32R) for b in range(2)]
        branch_lo = [sb(f"branch_lo{b}", [NC, SEQ], F32R) for b in range(2)]
        convin_a = sb("convin_a", [NC, KA - 1 + SEQ])
        convin_b = sb("convin_b", [NC, KB - 1 + SEQ])
        conv_a = sb("conv_a", [NC, SEQ])
        conv_b = sb("conv_b", [NC, SEQ])
        ln_sum = sb("ln_sum", [SEQ])
        ln_sd = sb("ln_sd", [SEQ])
        ln_rstd = sb("ln_rstd", [SEQ])
        params_in = [[sb(f"params_in{l}{j}", [P]) for j in range(2)] for l in range(2)]
        params = [sb(f"params{l}", [NPAR]) for l in range(2)]
        gain = sb("gain", [D])
        ident = sb("ident", [P])
        mean_of = sb("mean_of", [P])
        ones = sb("ones", [P])
        before = sb("before", [P])
        sumsq = sb("sumsq", [10])
        rstd = sb("rstd", [10])
        newton = sb("newton", [10])
        ln_eps = sb("ln_eps", [1])
        router = sb("router", [KD, E])
        router_parts = sb("router_parts", [KD, 2, E], F32R)
        earlier = sb("earlier", [E, E])
        iota_e = sb("iota_e", [E])
        iota_s = sb("iota_s", [SEQ])
        logits = sb("logits", [TT, E])
        pair_gt = sb("pair_gt", [TT, E, E])
        pair_eq = sb("pair_eq", [TT, E, E])
        rank = sb("rank", [TT, E])
        chosen = sb("chosen", [TT, E])
        top = sb("top", [TT])
        prob = sb("prob", [TT, E])
        total = sb("total", [TT])
        route = sb("route", [E, 2 * TT])
        place = sb("place", [TT, E])
        over = sb("over", [E])
        over_before = sb("over_before", [E])
        over_pairs = sb("over_pairs", [E, E])
        over_index = sb("over_index", [E])
        items_f = sb("items_f", [1 + 2 * E])
        items = sb("items", [1 + 2 * E], I32)
        cur = sb("cur", [2 * TT])
        cur_weight = sb("cur_weight", [TT])
        sel = sb("sel", [TT, P])
        selT = sb("selT", [SEQ], F32R)
        silu = gates
        g_tok = a_tok
        gT_hi, gT_lo = branch_hi[0], branch_lo[0]
        y_hi, y_lo = (m[1].rearrange("p c n -> p (c n)") for m in (branch_hi, branch_lo))

        ps = ctx.enter_context(nc.psum_tensor("ps", [P, 8, BANK], F32))

        raw_landed = [sem(f"raw_landed{s}") for s in range(RAW_SLOTS)]
        unit_hi = sem("unit_hi")
        unit_lo = sem("unit_lo")
        unit_done = sem("unit_done")
        params_landed = sem("params_landed")
        x_landed = [sem(f"x_landed{t}") for t in range(2)]
        router_landed = sem("router_landed")
        first_gain_landed = sem("first_gain_landed")
        gain_landed = sem("gain_landed")
        pool_step = sem("pool_step")
        consts_ready = sem("consts_ready")
        pads_ready = sem("pads_ready")
        paramsT_done = sem("paramsT_done")
        params_ready = sem("params_ready")
        sumsq_ready = sem("sumsq_ready")
        h_ready = sem("h_ready")
        tT_done = sem("tT_done")
        tT_hi = sem("tT_hi")
        tT_lo = sem("tT_lo")
        sig_ready = sem("sig_ready")
        a_ready = sem("a_ready")
        aT_done = sem("aT_done")
        convin_a_ready = sem("convin_a_ready")
        c_ready = sem("c_ready")
        v_ready = sem("v_ready")
        vT_done = sem("vT_done")
        convin_b_ready = sem("convin_b_ready")
        b_ready = sem("b_ready")
        bT_done = sem("bT_done")
        gate_ready = sem("gate_ready")
        conv_a_dve = sem("conv_a_dve")
        conv_b_dve = sem("conv_b_dve")
        tap_ready = sem("tap_ready")
        tap_added = sem("tap_added")
        ub_ready = sem("ub_ready")
        branch_hi_ready = [sem(f"branch_hi_ready{b}") for b in range(2)]
        branch_lo_ready = [sem(f"branch_lo_ready{b}") for b in range(2)]
        ln_sum_ready = sem("ln_sum_ready")
        mean_done = sem("mean_done")
        centred = sem("centred")
        squares_ready = sem("squares_ready")
        var_done = sem("var_done")
        ln_sd_ready = sem("ln_sd_ready")
        normed = sem("normed")
        lnsilu_ready = sem("lnsilu_ready")
        ya_tile0_done = sem("ya_tile0_done")
        merged_ready = sem("merged_ready")
        res_tile0_done = sem("res_tile0_done")
        x_ready = sem("x_ready")
        dve_step = sem("dve_step")
        silu_ready = sem("silu_ready")
        g_ready = sem("g_ready")
        gT_done = sem("gT_done")
        gT_hi_ready = sem("gT_hi_ready")
        gT_lo_ready = sem("gT_lo_ready")
        router_hi_ready = sem("router_hi_ready")
        router_ready = sem("router_ready")
        logits_done = sem("logits_done")
        shifted_ready = sem("shifted_ready")
        exp_ready = sem("exp_ready")
        chosen_ready = sem("chosen_ready")
        count_done = sem("count_done")
        items_ready = sem("items_ready")
        cur_ready = sem("cur_ready")
        sel_ready = sem("sel_ready")
        gather_done = sem("gather_done")
        selT_done = sem("selT_done")
        selT_ready = sem("selT_ready")
        hsel_hi_ready = sem("hsel_hi_ready")
        hsel_lo_ready = sem("hsel_lo_ready")
        y_hi_ready = sem("y_hi_ready")
        y_lo_ready = sem("y_lo_ready")
        scatter_done = sem("scatter_done")
        stored = sem("stored")

        DVE_TILES = NC // 2
        ACT_TAPS = KA * (NC - DVE_TILES)
        TAP_SLOTS = TT * D // SEQ
        TAPS_PER_UNIT = TAP_SLOTS - 1

        def tap(n):
            return h.rearrange("p t d -> p (t d)")[:, SEQ * (n % TAP_SLOTS):SEQ * (n % TAP_SLOTS + 1)]

        RESIDUALS = 3
        COUNT_BANK = 6
        scatter_banks = ((2, 3), (5, 7))

        block = ctx.enter_context(nc.Block())

        def moe_unit(kind, i, c, u):
            if kind != "down":
                at = u + (0 if kind == "w1" else 2)
                return Unit(MOE0 + at, i) if isinstance(c, int) and c == 0 else Unit(MOE0 - 2 + at, i, c)
            if isinstance(c, int) and c == MOE_CHUNKS:
                return Unit(MOE0 + 6 * MOE_CHUNKS - 2 + u, i)
            return Unit(MOE0 + 2 + u, i, c)

        def items_of(eng):
            eng.wait_ge(items_ready, 1)
            return eng.value_load(items[0:1, 0:1], min_val=E, max_val=2 * E)

        def for_items(eng, start, body, prepared):
            start(0, prepared)
            with eng.Fori(0, E - 1) as i:
                body(i, lambda: (i + 1, i + 1, 0))
            body(E - 1, None)
            n = items_of(eng)
            with eng.If(n > E):
                with eng.Fori(E, n) as i:
                    start(i, 0)
                    body(i, None)
            return n

        norms = [ins[n] for n in ("l0_norm1", "l0_norm2", "l1_norm1", "l1_norm2", "final_norm")]

        def load_gain(eng, k):
            if k:
                eng.wait_ge(h_ready, 2 * k)
            eng.dma_start(gain[:, :], norms[k].rearrange("(a d) -> a d", a=1).to_broadcast([P, D])
                          ).then_inc(gain_landed if k else first_gain_landed, 16)

        @block.sync
        def _(eng):
            def load(u, src):
                if not u.first_raw_round:
                    eng.wait_ge(unit_lo, u.n - (RAW_SLOTS - 1))
                k = src.shape[1]
                dst = raw[u.raw][:, 0:k * src.shape[2]].rearrange("p (k n) -> p k n", k=k)
                eng.dma_start(dst, src).then_inc(raw_landed[u.raw], 16)

            x_rows = x_in.rearrange("b (t p) d -> p (b t) d", p=P)
            eng.dma_start(x[:, 0, :], x_rows[:, 0, :]).then_inc(x_landed[0], 16)
            for n, src in enumerate(static_units):
                load(Unit(n), src)
                if n == 0:
                    load_gain(eng, 0)
                    eng.dma_start(x[:, 1, :], x_rows[:, 1, :]).then_inc(x_landed[1], 16)

            def item(i, e):
                def up(c):
                    for w, kind in zip(moe_up, ("w1", "w3")):
                        for u in range(2):
                            cols = slice(0, BANK) if isinstance(c, int) else bass.ds(c * BANK, BANK)
                            load(moe_unit(kind, i, c, u), w[e, :, 4 * u:4 * u + 4, cols])

                def down(c):
                    for u in range(2):
                        load(moe_unit("down", i, c, u), moe_down[e, :, bass.ds(4 * (c - 1) + 2 * u, 2), :])

                up(0)
                with eng.Fori(1, MOE_CHUNKS) as c:
                    up(c)
                    down(c)
                down(MOE_CHUNKS)

            with eng.Fori(0, E) as i:
                item(i, i)
            n = items_of(eng)
            with eng.If(n > E):
                with eng.Fori(E, n) as i:
                    item(i, eng.value_load(items[0:1, bass.ds(i + 1, 1)], min_val=0, max_val=E - 1))
            for t in range(TT):
                eng.wait_ge(h_ready, 2 * 4 + t + 1)
                eng.dma_start(out.rearrange("b (t p) d -> p (b t) d", p=P)[:, t, :],
                              h[:, t, :]).then_inc(stored, 16)
            eng.wait_ge(stored, 32)

        @block.gpsimd
        def _(eng):
            step = [0]

            def done(ins_):
                step[0] += 1
                ins_.then_inc(pool_step, 1)
                eng.wait_ge(pool_step, step[0])

            done(eng.memset(ident[:, :], 0.0))
            done(eng.affine_select(out=ident[:, :], in_=ident[:, :], compare_op=ALU.not_equal, fill=1.0,
                                   base=0, pattern=[[-1, P]], channel_multiplier=1))
            done(eng.memset(before[:, :], 0.0))
            done(eng.affine_select(out=before[:, :], in_=before[:, :], compare_op=ALU.is_ge, fill=1.0,
                                   base=0, pattern=[[-1, P]], channel_multiplier=1))
            done(eng.memset(earlier[:, :, :], 0.0))
            done(eng.affine_select(out=earlier[:, :, :], in_=earlier[:, :, :], compare_op=ALU.is_ge, fill=1.0,
                                   base=0, pattern=[[-1, E], [1, E]], channel_multiplier=0))
            done(eng.iota(iota_e[:, :], [[1, E]], base=0, channel_multiplier=0, allow_small_or_imprecise_dtypes=True))
            done(eng.iota(iota_s[:, :], [[1, SEQ]], base=0, channel_multiplier=0, allow_small_or_imprecise_dtypes=True))
            eng.memset(mean_of[:, :], 1.0 / C).then_inc(consts_ready, 1)
            eng.memset(ones[:, :], 1.0).then_inc(consts_ready, 1)
            eng.memset(ln_eps[:, :], LN_EPS).then_inc(consts_ready, 1)
            eng.memset(convin_a[:, :, 0:KA - 1], 0.0).then_inc(pads_ready, 1)
            eng.memset(convin_b[:, :, 0:KB - 1], 0.0).then_inc(pads_ready, 1)

            for l in range(2):
                eng.dma_start(params_in[l][0][0:KA * NC, :],
                              ins[f"l{l}_conv_a"].rearrange("k (c p) -> (k c) p", p=P)).then_inc(params_landed, 16)
                at = 0
                for name in ("conv_a_bias", "ln_a_g", "ln_a_b"):
                    eng.dma_start(params_in[l][1][at:at + NC, :],
                                  ins[f"l{l}_{name}"].rearrange("(c p) -> c p", p=P)).then_inc(params_landed, 16)
                    at += NC
                eng.dma_start(params_in[l][1][at:at + KB * NC, :],
                              ins[f"l{l}_conv_b"].rearrange("k (c p) -> (k c) p", p=P)).then_inc(params_landed, 16)
            with nc.allow_non_contiguous_dma(reason="the router's rows are eight floats"):
                eng.dma_start(router[:, :, :], ins["l1_router"].rearrange("(k p) e -> p k e", p=P)
                              ).then_inc(router_landed, 16)

            def lo(u):
                eng.wait_ge(raw_landed[u.raw], u.loads * 16)
                eng.wait_ge(unit_hi, u.n + 1)
                eng.wait_ge(unit_lo, u.n)
                eng.tensor_tensor(w_lo[u.split][:, :], raw[u.raw][:, :], w_hi[u.split][:, :],
                                  ALU.subtract).then_inc(unit_lo, 1)

            for l in range(2):
                if l:
                    lo(Unit(LAYER_UNITS + 1))
                load_gain(eng, 2 * l + 1)
                if l:
                    eng.wait_ge(lnsilu_ready, NC * l)
                for n in range(ACT_TAPS):
                    c = DVE_TILES + n % (NC - DVE_TILES)
                    acc = conv_a[:, c, :]
                    if n < NC - DVE_TILES:
                        eng.wait_ge(tap_ready, ACT_TAPS * l + n + 1)
                        eng.tensor_scalar(acc, tap(n), params[l][:, BIAS + c:BIAS + c + 1], None,
                                          ALU.add).then_inc(tap_added, 1)
                    else:
                        eng.wait_ge(tap_added, ACT_TAPS * l + n + 1 - (NC - DVE_TILES))
                        eng.wait_ge(tap_ready, ACT_TAPS * l + n + 1)
                        eng.tensor_tensor(acc, acc, tap(n), ALU.add).then_inc(tap_added, 1)
                if l == 0:
                    lo(Unit(MIX_UNITS + 1))
                load_gain(eng, 2 * l + 2)

        @block.scalar
        def _(eng):
            def hi(u):
                eng.wait_ge(raw_landed[u.raw], u.loads * 16)
                if not u.first_round:
                    eng.wait_ge(unit_done, u.n - (SPLIT_SLOTS - 1))
                nc.scalar.activation(w_hi[u.split][:, :], raw[u.raw][:, :], ACT.Copy).then_inc(unit_hi, 1)

            def norm(k, t):
                if k == 0:
                    eng.wait_ge(x_landed[t], 16)
                elif k < 4:
                    eng.wait_ge(x_ready, 4 * (k - 1) + 2 * t + 2)
                nc.scalar.activation(h[:, t, :], x[:, t, :], ACT.Square, scale=float(D) ** -0.5,
                                     accum_out=sumsq[:, 2 * k + t:2 * k + t + 1]).then_inc(sumsq_ready, 1)

            def transposed_hi(r, t):
                for b in range(2):
                    eng.wait_ge(tT_done, 4 * r + 2 * t + b + 1)
                    nc.scalar.activation(actT_hi[:, 4 * b:4 * b + 4, P * t:P * t + P],
                                         ps[:, 4 + 2 * t + b, :].rearrange("p (k n) -> p k n", k=4),
                                         ACT.Copy).then_inc(tT_hi, 1)

            def norm_block(k, r, m):
                norm(k, 0)
                hi(Unit(m + 1))
                transposed_hi(r, 0)
                norm(k, 1)
                transposed_hi(r, 1)
                hi(Unit(m + 2))

            def chunk_banks(k):
                return 2 * (k % 3)

            def from_z(l, k, func, dst, ready, free=None):
                eng.wait_ge(unit_done, LAYER_UNITS * l + 2 * k + 2)
                if free is not None:
                    eng.wait_ge(*free)
                for t in range(TT):
                    last = nc.scalar.activation(dst(t), ps[:, chunk_banks(k) + t, :], func)
                    if ready is not gate_ready or t == TT - 1:
                        last.then_inc(ready, 1)

            def mixer(l):
                U = LAYER_UNITS * l
                made = [0]

                def taps(count):
                    for n in range(made[0], min(made[0] + count, ACT_TAPS)):
                        k, c = n // (NC - DVE_TILES), DVE_TILES + n % (NC - DVE_TILES)
                        if n == 0:
                            eng.wait_ge(convin_a_ready, TT * (l + 1))
                            eng.wait_ge(params_ready, 2)
                        if n >= TAP_SLOTS:
                            eng.wait_ge(tap_added, ACT_TAPS * l + n + 1 - TAP_SLOTS)
                        nc.scalar.activation(tap(n), convin_a[:, c, k:k + SEQ], ACT.Copy,
                                             scale=params[l][:, k * NC + c:k * NC + c + 1]).then_inc(tap_ready, 1)
                        made[0] = n + 1

                for j in range(3, 6):
                    hi(Unit(U + j))
                from_z(l, A_GATE, ACT.Sigmoid, lambda t: gates[:, t, BANK:2 * BANK], sig_ready,
                       (g_ready, GDENSE) if l else None)
                hi(Unit(U + 6))
                if l == 0:
                    for m in range(2):
                        eng.wait_ge(paramsT_done, m + 1)
                        nc.scalar.activation(params[m][:, :], ps[:, 6 + m, 0:NPAR], ACT.Copy).then_inc(params_ready, 1)
                hi(Unit(U + 7))
                from_z(l, S_C, ACT.Copy, lambda t: gates[:, t, 0:BANK], c_ready)
                for t in range(TT):
                    eng.wait_ge(aT_done, TT * l + t + 1)
                    if t == 0 and l == 0:
                        eng.wait_ge(pads_ready, 2)
                    if t == 0 and l:
                        eng.wait_ge(centred, l)
                    nc.scalar.activation(convin_a[:, :, KA - 1 + P * t:KA - 1 + P * t + P],
                                         ps[:, 6 + t, :].rearrange("p (c n) -> p c n", c=NC),
                                         ACT.Copy).then_inc(convin_a_ready, 1)
                for j in range(8, 12):
                    hi(Unit(U + j))
                    taps(TAPS_PER_UNIT)
                from_z(l, S_B, ACT.Copy, lambda t: b_tok[:, t, :], b_ready)
                for t in range(TT):
                    eng.wait_ge(vT_done, TT * l + t + 1)
                    if t == 0 and l:
                        eng.wait_ge(ub_ready, TT * l)
                    nc.scalar.activation(convin_b[:, :, KB - 1 + P * t:KB - 1 + P * t + P],
                                         ps[:, 6 + t, :].rearrange("p (c n) -> p c n", c=NC),
                                         ACT.Copy).then_inc(convin_b_ready, 1)
                for k in range(G0, NZ - 1):
                    for j in range(2):
                        hi(Unit(U + 2 * k + 2 + j))
                        taps(TAPS_PER_UNIT)
                    at = (k - G0) * BANK
                    from_z(l, k, ACT.Sigmoid, lambda t: gates[:, t, at:at + BANK], gate_ready,
                           (v_ready, TT * (l + 1)) if k == G0 else (a_ready, TT * (l + 1)))
                taps(ACT_TAPS)
                eng.wait_ge(ub_ready, TT * (l + 1))
                nc.scalar.activation(branch_hi[1][:, :, :], conv_b[:, :, :], ACT.Copy).then_inc(branch_hi_ready[1], 1)
                eng.wait_ge(centred, l + 1)
                nc.scalar.activation(a_tok[:, :, :].rearrange("p t n -> p (t n)"),
                                     conv_a[:, :, :].rearrange("p c n -> p (c n)"),
                                     ACT.Square).then_inc(squares_ready, 1)
                hi(Unit(U + U_WB))
                hi(Unit(U + U_WB + 1))
                at3 = 3 * BANK
                from_z(l, NZ - 1, ACT.Sigmoid, lambda t: gates[:, t, at3:at3 + BANK], gate_ready)
                eng.wait_ge(var_done, l + 1)
                eng.wait_ge(consts_ready, 3)
                nc.scalar.activation(ln_sd[:, :], ps[:, 7, 0:SEQ], ACT.Sqrt, bias=ln_eps[:, :]).then_inc(ln_sd_ready, 1)
                hi(Unit(U + U_WA))
                eng.wait_ge(normed, l + 1)
                act = v_tok[:, :, :].rearrange("p t n -> p (t n)")
                for c in range(NC):
                    nc.scalar.activation(act[:, SEQ * c:SEQ * (c + 1)], conv_a[:, c, :], ACT.Silu,
                                         bias=params[l][:, LNB + c:LNB + c + 1],
                                         scale=params[l][:, LNG + c:LNG + c + 1]).then_inc(lnsilu_ready, 1)
                eng.wait_ge(lnsilu_ready, NC * (l + 1))
                nc.scalar.activation(branch_hi[0][:, :, :].rearrange("p c n -> p (c n)"), act,
                                     ACT.Copy).then_inc(branch_hi_ready[0], 1)
                hi(Unit(U + U_WA + 1))
                hi(Unit(U + U_WO))
                transposed_hi(3 * l + 1, 0)
                hi(Unit(U + U_WO + 1))
                hi(Unit(U + U_WO + 2))
                transposed_hi(3 * l + 1, 1)
                hi(Unit(U + U_WO + 3))

            def chunk_silu(done_n, g, nt, width):
                eng.wait_ge(unit_done, done_n)
                if not (isinstance(g, int) and g == 0):
                    eng.wait_ge(g_ready, g)
                for t in range(nt):
                    nc.scalar.activation(silu[:, t, 0:width], ps[:, 4 + t, 0:width], ACT.Silu).then_inc(silu_ready, 1)

            def gT_high(g, nt, width):
                for t in range(nt):
                    eng.wait_ge(gT_done, g + t + 1)
                    k = width // P
                    nc.scalar.activation(gT_hi[:, 0:k, P * t:P * t + P],
                                         ps[:, 4 + t, 0:width].rearrange("p (k n) -> p k n", k=k),
                                         ACT.Copy).then_inc(gT_hi_ready, 1)

            def dense():
                F = MIX_UNITS
                hi(Unit(F + 3))
                chunk_silu(F + 2, 0, TT, BANK)
                for c in range(1, DENSE_CHUNKS):
                    b = F + 6 * c - 2
                    for j in range(4):
                        hi(Unit(b + j))
                    chunk_silu(b + 2, TT * c, TT, BANK)
                    hi(Unit(b + 4))
                    gT_high(TT * (c - 1), TT, BANK)
                    hi(Unit(b + 5))
                b = F + 6 * DENSE_CHUNKS - 2
                hi(Unit(b))
                hi(Unit(b + 1))
                chunk_silu(b + 1, TT * DENSE_CHUNKS, TT, BANK // 2)
                hi(Unit(b + 2))
                gT_high(TT * (DENSE_CHUNKS - 1), TT, BANK)
                hi(Unit(b + 3))
                hi(Unit(b + 4))
                gT_high(TT * DENSE_CHUNKS, TT, BANK // 2)

            norm(0, 0)
            hi(Unit(0))
            transposed_hi(0, 0)
            norm(0, 1)
            hi(Unit(1))
            transposed_hi(0, 1)
            hi(Unit(2))
            mixer(0)
            eng.wait_ge(router_landed, 16)
            nc.scalar.activation(router_parts[:, :, 0, :], router[:, :, :], ACT.Copy).then_inc(router_hi_ready, 1)
            hi(Unit(MIX_UNITS))
            norm_block(1, 2, MIX_UNITS)
            dense()
            hi(Unit(LAYER_UNITS))
            norm_block(2, 3, LAYER_UNITS)
            mixer(1)
            hi(Unit(MOE0))
            norm_block(3, 5, MOE0)
            eng.wait_ge(shifted_ready, 1)
            nc.scalar.activation(prob[:, :, :], logits[:, :, :], ACT.Exp).then_inc(exp_ready, 1)

            def up(i, c, skip=0):
                units = [moe_unit(kind, i, c, u) for kind in ("w1", "w3") for u in range(2)]
                for u in units[skip:]:
                    hi(u)
                chunk_silu(units[1].n + 1, i * MOE_CHUNKS + (c + GDENSE), 1, BANK)

            def gathered_hi(i):
                for b in range(2):
                    eng.wait_ge(gather_done, i * 2 + b + 1)
                    nc.scalar.activation(actT_hi[:, 4 * b:4 * b + 4, 0:P],
                                         ps[:, 2 + b, :].rearrange("p (k n) -> p k n", k=4),
                                         ACT.Copy).then_inc(hsel_hi_ready, 1)

            def y_high(i):
                eng.wait_ge(unit_done, moe_unit("down", i, MOE_CHUNKS, 1).n + 1)
                for b in range(2):
                    nc.scalar.activation(y_hi[:, BANK * b:BANK * (b + 1)], ps[:, b, :],
                                         ACT.Copy).then_inc(y_hi_ready, 1)

            def start(i, prepared):
                gathered_hi(i)
                up(i, 0, prepared)

            def body(i, following):
                def chunk(c):
                    up(i, c)
                    hi(moe_unit("down", i, c, 0))
                    gT_high(i * MOE_CHUNKS + (c + (GDENSE - 1)), 1, BANK)
                    hi(moe_unit("down", i, c, 1))

                chunk(1)
                eng.wait_ge(selT_done, i + 1)
                nc.scalar.activation(selT[:, :], ps[:, 5, 0:SEQ], ACT.Copy).then_inc(selT_ready, 1)
                with eng.Fori(2, MOE_CHUNKS) as c:
                    chunk(c)
                hi(moe_unit("down", i, MOE_CHUNKS, 0))
                gT_high(i * MOE_CHUNKS + (MOE_CHUNKS + GDENSE - 1), 1, BANK)
                if following is None:
                    hi(moe_unit("down", i, MOE_CHUNKS, 1))
                    y_high(i)
                else:
                    j = following()[0]
                    hi(moe_unit("down", i, MOE_CHUNKS, 1))
                    gathered_hi(j)
                    for u in range(2):
                        hi(moe_unit("w1", j, 0, u))
                    y_high(i)
                    up(j, 0, 2)

            n = for_items(eng, start, body, 3)
            for t in range(TT):
                eng.wait_ge(x_ready, n * 4 + (4 * RESIDUALS - 2 * (TT - 1 - t)))
                norm(4, t)

        @block.vector
        def _(eng):
            step = [0]

            def done(ins_):
                step[0] += 1
                ins_.then_inc(dve_step, 1)
                eng.wait_ge(dve_step, step[0])

            def lo(u):
                eng.wait_ge(raw_landed[u.raw], u.loads * 16)
                eng.wait_ge(unit_hi, u.n + 1)
                nc.vector.tensor_tensor(w_lo[u.split][:, :], raw[u.raw][:, :], w_hi[u.split][:, :],
                                        ALU.subtract).then_inc(unit_lo, 1)

            def norm(k, t):
                s = 2 * k + t
                eng.wait_ge(sumsq_ready, s + 1)
                a, y, w = (m[:, s:s + 1] for m in (sumsq, rstd, newton))
                done(nc.vector.tensor_scalar(a, a, RMS_EPS, 0.5, ALU.add, ALU.mult))
                done(nc.vector.tensor_scalar(y.bitcast(I32), a.bitcast(I32), -0.5, float(0x5F3759DF - (1 << 22)),
                                             ALU.mult, ALU.add))
                for n in range(3):
                    done(nc.vector.scalar_tensor_tensor(out=w, in0=y, scalar=a, in1=y, op0=ALU.mult, op1=ALU.mult))
                    if n < 2:
                        done(nc.vector.scalar_tensor_tensor(out=y, in0=w, scalar=-1.5, in1=y, op0=ALU.add, op1=ALU.mult))
                done(nc.vector.tensor_scalar(w, w, -1.0, 1.5, ALU.mult, ALU.add))
                done(nc.vector.tensor_tensor(y, y, w, ALU.mult))
                eng.wait_ge(*((gain_landed, 16 * k) if k else (first_gain_landed, 16)))
                nc.vector.scalar_tensor_tensor(out=h[:, t, :], in0=x[:, t, :], scalar=rstd[:, s:s + 1],
                                               in1=gain[:, :], op0=ALU.mult, op1=ALU.mult).then_inc(h_ready, 1)

            def residual(q, t, end):
                if t == 0:
                    eng.wait_ge(res_tile0_done, q + 1)
                else:
                    eng.wait_ge(unit_done, end)
                for b in range(2):
                    part = x[:, t, BANK * b:BANK * (b + 1)]
                    nc.vector.tensor_tensor(part, part, ps[:, 2 * t + b, :], ALU.add).then_inc(x_ready, 1)

            def transposed_lo(r, t):
                for b in range(2):
                    eng.wait_ge(tT_hi, 4 * r + 2 * t + b + 1)
                    part = slice(4 * b, 4 * b + 4), slice(P * t, P * t + P)
                    nc.vector.tensor_tensor(actT_lo[:, part[0], part[1]],
                                            ps[:, 4 + 2 * t + b, :].rearrange("p (k n) -> p k n", k=4),
                                            actT_hi[:, part[0], part[1]], ALU.subtract).then_inc(tT_lo, 1)

            def norm_block(k, r, m):
                residual(k - 1, 0, m)
                norm(k, 0)
                residual(k - 1, 1, m)
                transposed_lo(r, 0)
                norm(k, 1)
                if k == 3:
                    transposed_lo(r, 1)
                else:
                    transposed_lo(r, 1)
                    eng.wait_ge(unit_lo, m + 2)
                    lo(Unit(m + 2))

            def mixer(l):
                U = LAYER_UNITS * l
                par = params[l]

                def product(k, dst, tmp, tmp_ready, ready):
                    eng.wait_ge(unit_done, U + 2 * k + 2)
                    for t in range(TT):
                        eng.wait_ge(tmp_ready, TT * l + t + 1)
                        nc.vector.tensor_tensor(dst[:, t, :], ps[:, 2 * (k % 3) + t, :], tmp[:, t, :],
                                                ALU.mult).then_inc(ready, 1)

                taps = [(k, c) for k in range(KA) for c in range(DVE_TILES)]
                mine = []

                def conv_taps(n):
                    for _ in range(min(n, len(taps))):
                        k, c = taps.pop(0)
                        if not mine:
                            eng.wait_ge(convin_a_ready, TT * (l + 1))
                            eng.wait_ge(params_ready, 2)
                        if k:
                            eng.wait_ge(conv_a_dve, len(taps_all) * l + len(mine) + 1 - DVE_TILES)
                        src = convin_a[:, c, k:k + SEQ]
                        w = par[:, k * NC + c:k * NC + c + 1]
                        if k == 0:
                            ins_ = nc.vector.tensor_scalar(conv_a[:, c, :], src, w, par[:, BIAS + c:BIAS + c + 1],
                                                           ALU.mult, ALU.add)
                        else:
                            ins_ = nc.vector.scalar_tensor_tensor(out=conv_a[:, c, :], in0=src, scalar=w,
                                                                  in1=conv_a[:, c, :], op0=ALU.mult, op1=ALU.add)
                        ins_.then_inc(conv_a_dve, 1)
                        mine.append((k, c))

                taps_all = list(taps)
                for j in range(3, 6):
                    lo(Unit(U + j))
                product(A_VAL, a_tok, gates[:, :, BANK:2 * BANK], sig_ready, a_ready)
                for j in range(6, 9):
                    lo(Unit(U + j))
                conv_taps(8)
                lo(Unit(U + 9))
                product(S_X, v_tok, gates[:, :, 0:BANK], c_ready, v_ready)
                conv_taps(6)
                for j in range(10, U_WB):
                    lo(Unit(U + j))
                    conv_taps(6 if j < 14 else 10)
                    if j == 14:
                        eng.wait_ge(convin_b_ready, TT * (l + 1))
                        for k in range(KB):
                            for c in range(NC):
                                src = convin_b[:, c, k:k + SEQ]
                                w = par[:, CONVB + k * NC + c:CONVB + k * NC + c + 1]
                                if k == 0:
                                    ins_ = nc.vector.tensor_scalar(conv_b[:, c, :], src, w, None, ALU.mult)
                                else:
                                    eng.wait_ge(conv_b_dve, NC * (KB * l + k - 1) + c + 1)
                                    ins_ = nc.vector.scalar_tensor_tensor(out=conv_b[:, c, :], in0=src, scalar=w,
                                                                          in1=conv_b[:, c, :], op0=ALU.mult, op1=ALU.add)
                                ins_.then_inc(conv_b_dve, 1)
                conv_taps(len(taps))
                eng.wait_ge(conv_a_dve, DVE_TILES * KA * (l + 1))
                eng.wait_ge(tap_added, ACT_TAPS * (l + 1))
                nc.vector.tensor_reduce(ln_sum[:, :], conv_a[:, :, :].rearrange("p c n -> p n c"), AX.X,
                                        ALU.add).then_inc(ln_sum_ready, 1)
                eng.wait_ge(conv_b_dve, NC * KB * (l + 1))
                for t in range(TT):
                    eng.wait_ge(bT_done, TT * l + t + 1)
                    part = conv_b[:, :, P * t:P * t + P]
                    nc.vector.tensor_tensor(part, part, ps[:, 6 + t, :].rearrange("p (c n) -> p c n", c=NC),
                                            ALU.mult).then_inc(ub_ready, 1)
                eng.wait_ge(mean_done, l + 1)
                nc.vector.tensor_tensor(conv_a[:, :, :], conv_a[:, :, :],
                                        ps[:, 6:7, 0:SEQ].to_broadcast([P, NC, SEQ]),
                                        ALU.subtract).then_inc(centred, 1)
                eng.wait_ge(ub_ready, TT * (l + 1))
                eng.wait_ge(branch_hi_ready[1], l + 1)
                nc.vector.tensor_tensor(branch_lo[1][:, :, :], conv_b[:, :, :], branch_hi[1][:, :, :],
                                        ALU.subtract).then_inc(branch_lo_ready[1], 1)
                eng.wait_ge(squares_ready, l + 1)
                nc.vector.tensor_reduce(ln_sum[:, :], a_tok[:, :, :].rearrange("p t (c n) -> p n t c", n=SEQ), AX.XY,
                                        ALU.add).then_inc(ln_sum_ready, 1)
                lo(Unit(U + U_WB))
                lo(Unit(U + U_WB + 1))
                eng.wait_ge(ln_sd_ready, l + 1)
                done(nc.vector.reciprocal(ln_rstd[:, :], ln_sd[:, :]))
                eng.wait_ge(centred, l + 1)
                nc.vector.tensor_tensor(conv_a[:, :, :], conv_a[:, :, :],
                                        ln_rstd[:, :].rearrange("p (a n) -> p a n", a=1).to_broadcast([P, NC, SEQ]),
                                        ALU.mult).then_inc(normed, 1)
                lo(Unit(U + U_WA))
                eng.wait_ge(branch_hi_ready[0], l + 1)
                nc.vector.tensor_tensor(branch_lo[0][:, :, :].rearrange("p c n -> p (c n)"),
                                        v_tok[:, :, :].rearrange("p t n -> p (t n)"),
                                        branch_hi[0][:, :, :].rearrange("p c n -> p (c n)"),
                                        ALU.subtract).then_inc(branch_lo_ready[0], 1)
                lo(Unit(U + U_WA + 1))
                eng.wait_ge(unit_done, U + U_WA)
                eng.wait_ge(gate_ready, 4 * (l + 1))
                for t in range(TT):
                    for b in range(2):
                        done(nc.vector.tensor_tensor(h[:, t, BANK * b:BANK * (b + 1)], ps[:, 2 * t + b, :],
                                                     gates[:, t, D + BANK * b:D + BANK * (b + 1)], ALU.mult))
                for t in range(TT):
                    if t == 0:
                        eng.wait_ge(ya_tile0_done, l + 1)
                    else:
                        eng.wait_ge(unit_done, U + U_WO)
                    for b in range(2):
                        ga = gates[:, t, BANK * b:BANK * (b + 1)]
                        done(nc.vector.tensor_tensor(ga, ps[:, 4 + 2 * t + b, :], ga, ALU.mult))
                    nc.vector.tensor_tensor(h[:, t, :], h[:, t, :], gates[:, t, 0:D], ALU.add).then_inc(merged_ready, 1)
                    if t == 0:
                        lo(Unit(U + U_WO))
                        transposed_lo(3 * l + 1, 0)
                        lo(Unit(U + U_WO + 1))
                lo(Unit(U + U_WO + 2))
                transposed_lo(3 * l + 1, 1)
                lo(Unit(U + U_WO + 3))

            def chunk_g(done_n, g, nt, width):
                eng.wait_ge(unit_done, done_n)
                for t in range(nt):
                    eng.wait_ge(silu_ready, g + t + 1)
                    nc.vector.tensor_tensor(g_tok[:, t, 0:width], ps[:, 6 + t, 0:width], silu[:, t, 0:width],
                                            ALU.mult).then_inc(g_ready, 1)

            def gT_low(g, nt, width):
                k = width // P
                for t in range(nt):
                    eng.wait_ge(gT_hi_ready, g + t + 1)
                    nc.vector.tensor_tensor(gT_lo[:, 0:k, P * t:P * t + P],
                                            ps[:, 4 + t, 0:width].rearrange("p (k n) -> p k n", k=k),
                                            gT_hi[:, 0:k, P * t:P * t + P], ALU.subtract).then_inc(gT_lo_ready, 1)

            def dense():
                F = MIX_UNITS
                for j in range(3, 6):
                    lo(Unit(F + j))
                chunk_g(F + 4, 0, TT, BANK)
                for c in range(1, DENSE_CHUNKS):
                    b = F + 6 * c - 2
                    for j in range(2 if c == 1 else 0, 5):
                        lo(Unit(b + j))
                    gT_low(TT * (c - 1), TT, BANK)
                    lo(Unit(b + 5))
                    chunk_g(b + 4, TT * c, TT, BANK)
                b = F + 6 * DENSE_CHUNKS - 2
                for j in range(3):
                    lo(Unit(b + j))
                gT_low(TT * (DENSE_CHUNKS - 1), TT, BANK)
                lo(Unit(b + 3))
                chunk_g(b + 2, TT * DENSE_CHUNKS, TT, BANK // 2)
                lo(Unit(b + 4))
                gT_low(TT * DENSE_CHUNKS, TT, BANK // 2)

            def routing():
                v = nc.vector
                one = logits[:, :, :].rearrange("p t (e a) -> p t e a", a=1).to_broadcast([P, TT, E, E])
                other = logits[:, :, :].rearrange("p t (a j) -> p t a j", a=1).to_broadcast([P, TT, E, E])
                for t in range(TT):
                    eng.wait_ge(logits_done, t + 1)
                    parts = ps[:, 4 + t, 0:2 * E]
                    done(v.tensor_copy(logits[:, t, :], parts[:, E:2 * E]))
                    done(v.tensor_tensor(logits[:, t, :], parts[:, 0:E], logits[:, t, :], ALU.add))
                    done(v.tensor_tensor(pair_gt[:, t], other[:, t], one[:, t], ALU.is_gt))
                    done(v.tensor_tensor(pair_eq[:, t], other[:, t], one[:, t], ALU.is_equal))
                    done(v.tensor_tensor(pair_eq[:, t], pair_eq[:, t], earlier[:, :, :], ALU.mult))
                    done(v.tensor_tensor(pair_gt[:, t], pair_gt[:, t], pair_eq[:, t], ALU.add))
                    done(v.tensor_reduce(rank[:, t, :], pair_gt[:, t], AX.X, ALU.add))
                    v.tensor_scalar(chosen[:, t, :], rank[:, t, :], 1.5, None, ALU.is_lt).then_inc(chosen_ready, 1)
                done(v.tensor_reduce(top[:, :], logits[:, :, :], AX.X, ALU.max))
                v.tensor_tensor(logits[:, :, :], logits[:, :, :],
                                top[:, :].rearrange("p (t a) -> p t a", a=1).to_broadcast([P, TT, E]),
                                ALU.subtract).then_inc(shifted_ready, 1)
                eng.wait_ge(chosen_ready, TT)
                eng.wait_ge(exp_ready, 1)
                done(v.tensor_tensor(prob[:, :, :], prob[:, :, :], chosen[:, :, :], ALU.mult))
                done(v.tensor_reduce(total[:, :], prob[:, :, :], AX.X, ALU.add))
                done(v.reciprocal(total[:, :], total[:, :]))
                done(v.tensor_tensor(route[:, :, TT:2 * TT].rearrange("p e t -> p t e"), prob[:, :, :],
                                     total[:, :].rearrange("p (t a) -> p t a", a=1).to_broadcast([P, TT, E]), ALU.mult))
                eng.wait_ge(count_done, 1)
                done(v.scalar_tensor_tensor(out=place[:, :, :], in0=ps[:, 0:TT, 0:E],
                                            scalar=1.0, in1=chosen[:, :, :], op0=ALU.add, op1=ALU.mult))
                done(v.tensor_scalar(route[:, :, 0:TT].rearrange("p e t -> p t e"), place[:, :, :], -1.0, None, ALU.add))

            def overflow():
                v = nc.vector
                done(v.tensor_scalar(over[:, :], ps[:, COUNT_BANK, 0:E], float(P) + 0.5, None, ALU.is_gt))
                over_j = over[:, :].rearrange("p (a j) -> p a j", a=1).to_broadcast([P, E, E])
                done(v.tensor_tensor(over_pairs[:, :, :], over_j, earlier[:, :, :], ALU.mult))
                done(v.tensor_reduce(over_before[:, :], over_pairs[:, :, :], AX.X, ALU.add))
                done(v.tensor_tensor(over_index[:, :], over[:, :], iota_e[:, :], ALU.mult))
                done(v.tensor_tensor(over_pairs[:, :, :],
                                     iota_e[:, :].rearrange("p (e a) -> p e a", a=1).to_broadcast([P, E, E]),
                                     over_before[:, :].rearrange("p (a j) -> p a j", a=1).to_broadcast([P, E, E]),
                                     ALU.is_equal))
                done(v.tensor_tensor(over_pairs[:, :, :], over_pairs[:, :, :],
                                     over_index[:, :].rearrange("p (a j) -> p a j", a=1).to_broadcast([P, E, E]), ALU.mult))
                done(v.tensor_reduce(items_f[:, 1 + E:1 + 2 * E], over_pairs[:, :, :], AX.X, ALU.add))
                done(v.tensor_copy(items_f[:, 1:1 + E], iota_e[:, :]))
                done(v.tensor_reduce(items_f[:, 0:1], over[:, :], AX.X, ALU.add))
                done(v.tensor_scalar(items_f[:, 0:1], items_f[:, 0:1], float(E), None, ALU.add))
                v.tensor_copy(items[:, :], items_f[:, :]).then_inc(items_ready, 1)

            def select(i, e, group, read_by=None):
                if i is not e:
                    e = eng.value_load(items[0:1, bass.ds(i + 1, 1)], min_val=0, max_val=E - 1)
                if read_by is not None:
                    eng.wait_ge(cur_ready, read_by * 2 + 2)
                nc.vector.tensor_copy(cur[:, :].rearrange("p (a n) -> p a n", a=1),
                                      route[:, bass.ds(e, 1), :]).then_inc(cur_ready, 1)
                eng.wait_ge(cur_ready, i * 2 + 1)
                if read_by is not None:
                    eng.wait_ge(selT_done, read_by + 1)
                for t in range(TT):
                    nc.vector.tensor_scalar(sel[:, t, :], iota_s[:, P * group:P * group + P], cur[:, t:t + 1], None,
                                            ALU.is_equal).then_inc(sel_ready, 1)

            def gathered_lo(i):
                for b in range(2):
                    eng.wait_ge(hsel_hi_ready, i * 2 + b + 1)
                    nc.vector.tensor_tensor(actT_lo[:, 4 * b:4 * b + 4, 0:P],
                                            ps[:, 2 + b, :].rearrange("p (k n) -> p k n", k=4),
                                            actT_hi[:, 4 * b:4 * b + 4, 0:P], ALU.subtract).then_inc(hsel_lo_ready, 1)

            def y_low(i):
                for b in range(2):
                    part = slice(BANK * b, BANK * (b + 1))
                    eng.wait_ge(y_hi_ready, i * 2 + b + 1)
                    nc.vector.tensor_tensor(y_lo[:, part], ps[:, b, :], y_hi[:, part],
                                            ALU.subtract).then_inc(y_lo_ready, 1)

            def add_back(i, t):
                eng.wait_ge(cur_ready, i * 2 + 2)
                for b in range(2):
                    eng.wait_ge(scatter_done, i * 4 + 2 * t + b + 1)
                    part = x[:, t, BANK * b:BANK * (b + 1)]
                    nc.vector.scalar_tensor_tensor(out=part, in0=ps[:, scatter_banks[t][b], :],
                                                   scalar=cur_weight[:, t:t + 1], in1=part,
                                                   op0=ALU.mult, op1=ALU.add).then_inc(x_ready, 1)

            def up(i, c, skip=0, last=4):
                units = [moe_unit(kind, i, c, u) for kind in ("w1", "w3") for u in range(2)]
                for u in units[skip:last]:
                    lo(u)
                return units[3].n + 1

            def start(i, prepared):
                select(i, i if isinstance(i, int) else None, 0 if isinstance(i, int) else 1)
                if isinstance(i, int):
                    lo(Unit(MOE0 + 1))
                gathered_lo(i)
                if isinstance(i, int):
                    lo(Unit(MOE0 + 2))
                    overflow()
                first_g(i, up(i, 0, prepared))

            def first_g(i, n):
                for u in range(2):
                    lo(moe_unit("w1", i, 1, u))
                chunk_g(n, i * MOE_CHUNKS + GDENSE, 1, BANK)

            def body(i, following):
                def chunk(c, ahead=0):
                    n = up(i, c, ahead)
                    lo(moe_unit("down", i, c, 0))
                    gT_low(i * MOE_CHUNKS + (c + (GDENSE - 1)), 1, BANK)
                    lo(moe_unit("down", i, c, 1))
                    chunk_g(n, i * MOE_CHUNKS + (c + GDENSE), 1, BANK)

                chunk(1, 2)
                eng.wait_ge(x_ready, i * 4 + 4 * RESIDUALS)
                nc.vector.tensor_copy(cur_weight[:, :], cur[:, TT:2 * TT]).then_inc(cur_ready, 1)
                if following is not None:
                    select(*following(), read_by=i)
                with eng.Fori(2, MOE_CHUNKS) as c:
                    chunk(c)
                lo(moe_unit("down", i, MOE_CHUNKS, 0))
                gT_low(i * MOE_CHUNKS + (MOE_CHUNKS + GDENSE - 1), 1, BANK)
                if following is None:
                    lo(moe_unit("down", i, MOE_CHUNKS, 1))
                    y_low(i)
                    for t in range(TT):
                        add_back(i, t)
                else:
                    j = following()[0]
                    lo(moe_unit("down", i, MOE_CHUNKS, 1))
                    gathered_lo(j)
                    up(j, 0, 0, 2)
                    y_low(i)
                    up(j, 0, 2, 3)
                    add_back(i, 0)
                    n = up(j, 0, 3)
                    add_back(i, 1)
                    first_g(j, n)

            norm(0, 0)
            lo(Unit(0))
            transposed_lo(0, 0)
            norm(0, 1)
            lo(Unit(1))
            transposed_lo(0, 1)
            lo(Unit(2))
            mixer(0)
            eng.wait_ge(router_landed, 16)
            eng.wait_ge(router_hi_ready, 1)
            nc.vector.tensor_tensor(router_parts[:, :, 1, :], router[:, :, :], router_parts[:, :, 0, :],
                                    ALU.subtract).then_inc(router_ready, 1)
            lo(Unit(MIX_UNITS))
            norm_block(1, 2, MIX_UNITS)
            dense()
            lo(Unit(LAYER_UNITS))
            norm_block(2, 3, LAYER_UNITS)
            mixer(1)
            lo(Unit(MOE0))
            norm_block(3, 5, MOE0)
            routing()
            for_items(eng, start, body, 3)
            for t in range(TT):
                norm(4, t)

        @block.tensor
        def _(eng):
            mm = nc.tensor.matmul

            def product(dst, act, w, start, stop):
                (act_hi, act_lo), (wh, wl) = act, w
                mm(dst, act_hi, wh, start=start, stop=False)
                mm(dst, act_hi, wl, start=False, stop=False)
                return mm(dst, act_lo, wh, start=False, stop=stop)

            def weights(u, a, b):
                return w_hi[u.split][:, a:b], w_lo[u.split][:, a:b]

            def stationary(pair, k, t):
                return tuple(m[:, k, P * t:P * t + P] for m in pair)

            act = (actT_hi, actT_lo)
            gT = (gT_hi, gT_lo)

            def up_by_tile(n, r, bank):
                transposes(r, 0, h_ready, norm_of(r) * TT + 1)
                for t in range(TT):
                    for j in range(2):
                        u = Unit(n + j)
                        eng.wait_ge(tT_lo, 4 * r + 2 * t + j + 1)
                        eng.wait_ge(unit_lo, u.n + 1)
                        for q in range(4):
                            last = product(ps[:, bank + t, :], stationary(act, 4 * j + q, t),
                                           weights(u, BANK * q, BANK * (q + 1)),
                                           start=(j == 0 and q == 0), stop=(j == 1 and q == 3))
                        if t == TT - 1:
                            last.then_inc(unit_done, 1)
                        elif j == 0:
                            transposes(r, 1, h_ready, norm_of(r) * TT + 2)

            def up_unit(u, j, bank, nt, width=BANK, halfway=None):
                eng.wait_ge(unit_lo, u.n + 1)
                k = UNIT // width
                for q in range(k):
                    if halfway is not None and q == k // 2:
                        halfway()
                    for t in range(nt):
                        last = product(ps[:, bank + t, 0:width], stationary(act, k * j + q, t),
                                       weights(u, width * q, width * (q + 1)),
                                       start=(j == 0 and q == 0), stop=(k * j + q == KD - 1))
                last.then_inc(unit_done, 1)

            def norm_of(r):
                return {0: 0, 2: 1, 3: 2, 5: 3}[r]

            def transposes(r, t, ready, value):
                eng.wait_ge(ready, value)
                for k in range(KD):
                    last = nc.tensor.transpose(ps[:, 4 + 2 * t + k // 4, P * (k % 4):P * (k % 4) + P],
                                               h[:, t, P * k:P * k + P], ident[:, :])
                    if k % 4 == 3:
                        last.then_inc(tT_done, 1)

            def channel_transposes(src, l, ready, done_sem):
                for t in range(TT):
                    eng.wait_ge(ready, TT * l + t + 1)
                    for c in range(NC):
                        last = nc.tensor.transpose(ps[:, 6 + t, P * c:P * c + P], src[:, t, P * c:P * c + P], ident[:, :])
                    last.then_inc(done_sem, 1)

            def mixer(l):
                U = LAYER_UNITS * l

                def z(k):
                    for j in range(2):
                        up_unit(Unit(U + 2 * k + j), j, 2 * (k % 3), TT)

                up_by_tile(U, 3 * l, 0)
                z(A_GATE)
                if l == 0:
                    eng.wait_ge(params_landed, 16 * 10)
                    for m in range(2):
                        a, b = params_in[m]
                        nb = NPAR - KA * NC
                        nc.tensor.transpose(ps[:, 6 + m, 0:KA * NC], a[0:KA * NC, :], ident[0:KA * NC, 0:KA * NC])
                        nc.tensor.transpose(ps[:, 6 + m, KA * NC:NPAR], b[0:nb, :], ident[0:nb, 0:nb]).then_inc(paramsT_done, 1)
                z(S_C)
                if l == 0:
                    eng.wait_ge(params_ready, 2)
                channel_transposes(a_tok, l, a_ready, aT_done)
                z(S_X)
                z(S_B)
                eng.wait_ge(convin_a_ready, TT * (l + 1))
                channel_transposes(v_tok, l, v_ready, vT_done)
                z(G0)
                eng.wait_ge(convin_b_ready, TT * (l + 1))
                channel_transposes(b_tok, l, b_ready, bT_done)
                z(G0 + 1)
                z(G0 + 2)
                eng.wait_ge(gate_ready, 4 * l + 1)
                up_unit(Unit(U + 2 * NZ - 2), 0, 2 * ((NZ - 1) % 3), TT)
                eng.wait_ge(ln_sum_ready, 2 * l + 1)
                eng.wait_ge(ub_ready, TT * l + 1)
                mm(ps[:, 6, 0:SEQ], mean_of[:, :], ln_sum[:, :], start=True, stop=True).then_inc(mean_done, 1)
                up_unit(Unit(U + 2 * NZ - 1), 1, 2 * ((NZ - 1) % 3), TT)
                eng.wait_ge(ub_ready, TT * (l + 1))
                eng.wait_ge(ln_sum_ready, 2 * l + 2)
                mm(ps[:, 7, 0:SEQ], mean_of[:, :], ln_sum[:, :], start=True, stop=True).then_inc(var_done, 1)
                branch = [(branch_hi[b], branch_lo[b]) for b in range(2)]
                eng.wait_ge(gate_ready, 4 * l + 3)
                eng.wait_ge(branch_lo_ready[1], l + 1)
                for j in range(2):
                    u = Unit(U + U_WB + j)
                    eng.wait_ge(unit_lo, u.n + 1)
                    for q in range(2):
                        for t in range(TT):
                            for b in range(2):
                                last = product(ps[:, 2 * t + b, :], stationary(branch[1], 2 * j + q, t),
                                               weights(u, D * q + BANK * b, D * q + BANK * (b + 1)),
                                               start=(j == 0 and q == 0), stop=(j == 1 and q == 1))
                    last.then_inc(unit_done, 1)
                eng.wait_ge(gate_ready, 4 * l + 4)
                eng.wait_ge(normed, l + 1)
                eng.wait_ge(branch_lo_ready[0], l + 1)
                for t in range(TT):
                    for j in range(2):
                        if t and j:
                            transposes(3 * l + 1, 0, merged_ready, TT * l + 1)
                        last = down_tile(U + U_WA + j, branch[0], 2 * j, t, 4, j == 0, j == 1)
                        if t:
                            last.then_inc(unit_done, 1)
                    if t == 0:
                        last.then_inc(ya_tile0_done, 1)
                for t, j in ((0, 0), (0, 1), (0, 2), (1, 0), (1, 1), (0, 3), (1, 2), (1, 3)):
                    if (t, j) == (0, 2):
                        transposes(3 * l + 1, 1, merged_ready, TT * l + 2)
                    if j in (0, 2):
                        eng.wait_ge(tT_lo, 4 * (3 * l + 1) + 2 * t + j // 2 + 1)
                    last = down_tile(U + U_WO + j, act, 2 * j, t, 0, j == 0, j == 3)
                    if t:
                        last.then_inc(unit_done, 1)
                    elif j == 3:
                        last.then_inc(res_tile0_done, 1)

            def down_tile(n, left, k0, t, bank, first, final):
                u = Unit(n)
                eng.wait_ge(unit_lo, n + 1)
                for q in range(2):
                    for b in range(2):
                        last = product(ps[:, bank + 2 * t + b, :], stationary(left, k0 + q, t),
                                       weights(u, D * q + BANK * b, D * q + BANK * (b + 1)),
                                       start=first and q == 0, stop=final and q == 1)
                return last

            def g_transposes(g, nt, width, silu_count):
                if silu_count is not None:
                    eng.wait_ge(silu_ready, silu_count)
                for t in range(nt):
                    eng.wait_ge(g_ready, g + t + 1)
                    for k in range(width // P):
                        last = nc.tensor.transpose(ps[:, 4 + t, P * k:P * k + P], g_tok[:, t, P * k:P * k + P], ident[:, :])
                    last.then_inc(gT_done, 1)

            def dense():
                F = MIX_UNITS
                up_by_tile(F, 2, 4)
                for j in range(2):
                    up_unit(Unit(F + 2 + j), j, 6, TT)
                for c in range(1, DENSE_CHUNKS):
                    b = F + 6 * c - 2
                    for j in range(2):
                        up_unit(Unit(b + j), j, 4, TT)
                    eng.wait_ge(g_ready, TT * c)
                    up_unit(Unit(b + 2), 0, 6, TT)
                    g_transposes(TT * (c - 1), TT, BANK, TT * (c + 1))
                    up_unit(Unit(b + 3), 1, 6, TT)
                    eng.wait_ge(gT_lo_ready, TT * c)
                    dense_down(b + 4, c == 1, False)
                b = F + 6 * DENSE_CHUNKS - 2
                up_unit(Unit(b), 0, 4, TT, BANK // 2)
                eng.wait_ge(g_ready, TT * DENSE_CHUNKS)
                up_unit(Unit(b + 1), 0, 6, TT, BANK // 2,
                        lambda: g_transposes(TT * (DENSE_CHUNKS - 1), TT, BANK, TT * (DENSE_CHUNKS + 1)))
                eng.wait_ge(gT_lo_ready, TT * DENSE_CHUNKS)
                dense_down(b + 2, False, False, 1)
                g_transposes(TT * DENSE_CHUNKS, TT, BANK // 2, None)
                for t in range(TT):
                    last = down_tile(b + 3, gT, 2, t, 0, False, False)
                    if t:
                        last.then_inc(unit_done, 1)
                    eng.wait_ge(gT_lo_ready, TT * DENSE_CHUNKS + t + 1)
                    down_tile(b + 4, gT, 0, t, 0, False, True).then_inc(unit_done if t else res_tile0_done, 1)

            def dense_down(n, first, final, count=2):
                for j in range(count):
                    u = Unit(n + j)
                    eng.wait_ge(unit_lo, u.n + 1)
                    for q in range(2):
                        for t in range(TT):
                            for b in range(2):
                                last = product(ps[:, 2 * t + b, :], stationary(gT, 2 * j + q, t),
                                               weights(u, D * q + BANK * b, D * q + BANK * (b + 1)),
                                               start=first and j == 0 and q == 0, stop=final)
                    last.then_inc(unit_done, 1)

            def routing():
                transposes(5, 0, h_ready, 3 * TT + 1)
                eng.wait_ge(router_ready, 1)
                def count(bank, of, t, first, last):
                    return mm(ps[:, bank, 0:E], of[:, :], chosen[:, t, :], start=first, stop=last)

                for t in range(TT):
                    for k in range(KD):
                        if k % 4 == 0:
                            eng.wait_ge(tT_lo, 4 * 5 + 2 * t + k // 4 + 1)
                        for a, left in enumerate((actT_hi, actT_lo)):
                            last = mm(ps[:, 4 + t, 0:2 * E], left[:, k, P * t:P * t + P],
                                      router_parts[:, k, :, :].rearrange("p a e -> p (a e)"),
                                      start=(k == a == 0), stop=(k == KD - 1 and a == 1))
                    last.then_inc(logits_done, 1)
                    if t == 0:
                        transposes(5, 1, h_ready, 3 * TT + 2)
                eng.wait_ge(chosen_ready, 1)
                count(0, before, 0, True, True)
                count(1, ones, 0, True, False)
                count(COUNT_BANK, ones, 0, True, False)
                eng.wait_ge(chosen_ready, 2)
                count(1, before, 1, False, True)
                count(COUNT_BANK, ones, 1, False, True).then_inc(count_done, 1)

            def gather(i, b):
                if b == 0:
                    eng.wait_ge(sel_ready, i * TT + TT)
                for k in range(4 * b, 4 * b + 4):
                    for t in range(TT):
                        last = mm(ps[:, 2 + b, P * (k % 4):P * (k % 4) + P], h[:, t, P * k:P * k + P], sel[:, t, :],
                                  start=(t == 0), stop=(t == TT - 1))
                last.then_inc(gather_done, 1)

            def g_of(i, c):
                return i * MOE_CHUNKS + (c + GDENSE)

            def down(i, c, first, final=False):
                eng.wait_ge(gT_lo_ready, g_of(i, c))
                for j in range(2):
                    u = moe_unit("down", i, c, j)
                    eng.wait_ge(unit_lo, u.n + 1)
                    for q in range(2):
                        for b in range(2):
                            last = product(ps[:, b, :], stationary(gT, 2 * j + q, 0),
                                           weights(u, D * q + BANK * b, D * q + BANK * (b + 1)),
                                           start=first and j == 0 and q == 0,
                                           stop=final and j == 1 and q == 1)
                    last.then_inc(unit_done, 1)

            def up_w1(i, c):
                for j in range(2):
                    up_unit(moe_unit("w1", i, c, j), j, 4, 1)

            def up_w3(i, c):
                eng.wait_ge(g_ready, g_of(i, c))
                up_unit(moe_unit("w3", i, c, 0), 0, 6, 1)
                if not isinstance(c, int) or c:
                    g_transposes(g_of(i, c) - 1, 1, BANK, g_of(i, c) + 1)
                up_unit(moe_unit("w3", i, c, 1), 1, 6, 1)

            def scatter(i):
                eng.wait_ge(selT_ready, i + 1)
                for t in range(TT):
                    for b in range(2):
                        if t == 0:
                            eng.wait_ge(y_lo_ready, i * 2 + b + 1)
                        for y in (y_hi, y_lo):
                            last = mm(ps[:, scatter_banks[t][b], :], selT[:, P * t:P * t + P],
                                      y[:, BANK * b:BANK * (b + 1)], start=y is y_hi, stop=y is y_lo)
                        last.then_inc(scatter_done, 1)

            def start(i, prepared):
                gather(i, 0)
                gather(i, 1)
                eng.wait_ge(hsel_lo_ready, i * 2 + 2)
                up_w1(i, 0)
                if isinstance(i, int):
                    eng.wait_ge(items_ready, 1)
                up_w3(i, 0)

            def body(i, following):
                up_w1(i, 1)
                up_w3(i, 1)
                eng.wait_ge(x_ready, i * 4 + 4 * RESIDUALS)
                for t in range(TT):
                    last = nc.tensor.transpose(ps[:, 5, P * t:P * t + P], sel[:, t, :], ident[:, :])
                last.then_inc(selT_done, 1)
                down(i, 1, True)
                with eng.Fori(2, MOE_CHUNKS) as c:
                    up_w1(i, c)
                    up_w3(i, c)
                    down(i, c, False)
                if following is None:
                    g_transposes(g_of(i, MOE_CHUNKS - 1), 1, BANK, None)
                    down(i, MOE_CHUNKS, False, True)
                    scatter(i)
                else:
                    j = following()[0]
                    g_transposes(g_of(i, MOE_CHUNKS - 1), 1, BANK, None)
                    gather(j, 0)
                    gather(j, 1)
                    down(i, MOE_CHUNKS, False, True)
                    eng.wait_ge(hsel_lo_ready, j * 2 + 2)
                    up_w1(j, 0)
                    scatter(i)
                    up_w3(j, 0)

            eng.wait_ge(pool_step, 2)
            eng.wait_ge(consts_ready, 3)
            mixer(0)
            dense()
            mixer(1)
            routing()
            for_items(eng, start, body, 3)


def kernel(**inputs):
    import numpy as np
    from concourse import bacc
    from concourse.bass_utils import run_bass_kernel_spmd

    nc = bacc.Bacc("TRN2", target_bir_lowering=False, num_devices=1)
    arrays, ins = {}, {}
    for name, value in inputs.items():
        a = np.ascontiguousarray(value)
        arrays[f"in_{name}"] = a
        ins[name] = nc.dram_tensor(f"in_{name}", a.shape, mybir.dt.from_np(a.dtype), kind="ExternalInput").ap()
    out = nc.dram_tensor("out", inputs["x"].shape, F32, kind="ExternalOutput").ap()
    trunk(nc, ins, out)
    result = run_bass_kernel_spmd(nc, [arrays], core_ids=[0])
    return result.results[0]["out"]
```
